# Optimizing a Trainium2 kernel written in Bass

```python
import math
import jax
import jax.numpy as jnp
from jax import lax
import numpy as np

D_MODEL = 1024
BATCH = 1
SEQ = 1024
DEPTH = 2

GRID_W = 64
CTX_LEN = 256
N_MIXERS = 2
WIDTH = D_MODEL
NA_HEADS = 16
NA_HEAD_DIM = WIDTH // NA_HEADS
NA_WIN_R = 8
NA_WIN_C = 16
DIFF_HEADS = 8
DIFF_HEAD_DIM = WIDTH // (2 * DIFF_HEADS)
Q_BLOCK = 128
ROPE_BASE = 10000.0
LN_EPS = 1e-5
DEEPNORM_ALPHA = (2.0 * DEPTH) ** 0.25
DEEPNORM_BETA = (8.0 * DEPTH) ** -0.25
N_NA_LAYERS = (DEPTH + 1) // 2
N_DIFF_LAYERS = DEPTH // 2

kernel_name = 'hybrid_natten_diffattn_dit'

def _layer_norm(x, g, b):
    xf = x.astype(jnp.float32)
    mu = jnp.mean(xf, axis=-1, keepdims=True)
    var = jnp.mean(jnp.square(xf - mu), axis=-1, keepdims=True)
    return ((xf - mu) * lax.rsqrt(var + LN_EPS)).astype(x.dtype) * g + b

def _rms_norm(x, g):
    xf = x.astype(jnp.float32)
    ms = jnp.mean(jnp.square(xf), axis=-1, keepdims=True)
    return (xf * lax.rsqrt(ms + LN_EPS)).astype(x.dtype) * g

def _modulation(cond, w_mod, b_mod):
    m = jax.nn.silu(cond) @ w_mod + b_mod
    return jnp.split(m, 3, axis=-1)

def _split_heads(t, n_heads):
    b, n, _ = t.shape
    return t.reshape(b, n, n_heads, -1).transpose(0, 2, 1, 3)

def _merge_heads(t):
    b, h, n, d = t.shape
    return t.transpose(0, 2, 1, 3).reshape(b, n, h * d)

def _softmax_attend(q, k, v, scale):
    s = jnp.einsum('bhqd,bhkd->bhqk', q, k).astype(jnp.float32) * scale
    p = jax.nn.softmax(s, axis=-1).astype(v.dtype)
    return jnp.einsum('bhqk,bhkd->bhqd', p, v)

def _axial_rope_tables(n_tok):
    t = jnp.arange(n_tok, dtype=jnp.int32)
    pos = jnp.stack([t // GRID_W, t % GRID_W], axis=-1).astype(jnp.float32)
    n_freq = DIFF_HEAD_DIM // 4
    inv_freq = ROPE_BASE ** (-jnp.arange(n_freq, dtype=jnp.float32) / n_freq)
    ang = pos[:, :, None] * inv_freq
    return jnp.cos(ang), jnp.sin(ang)

def _apply_axial_rope(x, cos, sin):
    shp = x.shape
    xr = x.reshape(shp[:-1] + (2, 2, shp[-1] // 4))
    x1, x2 = xr[..., 0, :], xr[..., 1, :]
    cos = cos.astype(x.dtype)
    sin = sin.astype(x.dtype)
    out = jnp.stack([x1 * cos - x2 * sin, x2 * cos + x1 * sin], axis=-2)
    return out.reshape(shp)

def _na_mixer(q, k, v, qc, kc, vc, rpb, need_ctx):
    q, k, v = _split_heads(q, NA_HEADS), _split_heads(k, NA_HEADS), _split_heads(v, NA_HEADS)
    kc, vc = _split_heads(kc, NA_HEADS), _split_heads(vc, NA_HEADS)
    b, h, n, d = q.shape
    rows = n // GRID_W
    kr = min(NA_WIN_R, rows)
    n_win = kr * NA_WIN_C
    scale = d ** -0.5
    kg = k.reshape(b, h, rows, GRID_W, d)
    vg = v.reshape(b, h, rows, GRID_W, d)
    q_rows = jnp.moveaxis(q.reshape(b, h, rows, GRID_W, d), 2, 0)
    r_idx = jnp.arange(rows, dtype=jnp.int32)
    row_start = jnp.clip(r_idx - kr // 2, 0, rows - kr)
    w_idx = jnp.arange(GRID_W, dtype=jnp.int32)
    col_start = jnp.clip(w_idx - NA_WIN_C // 2, 0, GRID_W - NA_WIN_C)
    col_idx = col_start[:, None] + jnp.arange(NA_WIN_C, dtype=jnp.int32)
    rpb_cols = rpb[:, :, col_idx - w_idx[:, None] + NA_WIN_C - 1]

    def row_block(args):
        q_r, r, r0 = args
        k_win = lax.dynamic_slice_in_dim(kg, r0, kr, axis=2)[:, :, :, col_idx, :]
        v_win = lax.dynamic_slice_in_dim(vg, r0, kr, axis=2)[:, :, :, col_idx, :]
        bias = rpb_cols[:, r0 + jnp.arange(kr, dtype=jnp.int32) - r + NA_WIN_R - 1]
        s_loc = (jnp.einsum('bhwd,bhiwjd->bhwij', q_r, k_win).astype(jnp.float32) * scale
                 + bias.transpose(0, 2, 1, 3).astype(jnp.float32))
        s_ctx = jnp.einsum('bhwd,bhcd->bhwc', q_r, kc).astype(jnp.float32) * scale
        s = jnp.concatenate([s_loc.reshape(b, h, GRID_W, n_win), s_ctx], axis=-1)
        p = jax.nn.softmax(s, axis=-1).astype(v.dtype)
        p_loc = p[..., :n_win].reshape(b, h, GRID_W, kr, NA_WIN_C)
        return (jnp.einsum('bhwij,bhiwjd->bhwd', p_loc, v_win)
                + jnp.einsum('bhwc,bhcd->bhwd', p[..., n_win:], vc))

    y = lax.map(row_block, (q_rows, r_idx, row_start))
    y = jnp.moveaxis(y, 0, 2).reshape(b, h, n, d)
    y_ctx = None
    if need_ctx:
        y_ctx = _merge_heads(_softmax_attend(_split_heads(qc, NA_HEADS), kc, vc, scale))
    return _merge_heads(y), y_ctx

def _diff_heads(t):
    b, n, _ = t.shape
    return t.reshape(b, n, DIFF_HEADS, 2, DIFF_HEAD_DIM).transpose(0, 2, 3, 1, 4)

def _diff_core(q, k, v, lam, scale):
    s = jnp.einsum('bhmqd,bhmkd->bhmqk', q, k).astype(jnp.float32) * scale
    p = jax.nn.softmax(s, axis=-1)
    a = (p[:, :, 0] - lam * p[:, :, 1]).astype(v.dtype)
    return jnp.einsum('bhqk,bhkv->bhqv', a, v)

def _diff_mixer(q, k, v, qc, kc, vc, lam_params, subln_g, lambda_init, cos, sin, need_ctx):
    scale = DIFF_HEAD_DIM ** -0.5
    lp = lam_params.astype(jnp.float32)
    lam = jnp.exp(jnp.sum(lp[0] * lp[1])) - jnp.exp(jnp.sum(lp[2] * lp[3])) + lambda_init
    q = _apply_axial_rope(_diff_heads(q), cos, sin)
    k = _apply_axial_rope(_diff_heads(k), cos, sin)
    v = _split_heads(v, DIFF_HEADS)
    kc = _diff_heads(kc)
    vc = _split_heads(vc, DIFF_HEADS)
    k_all = jnp.concatenate([k, kc], axis=3)
    v_all = jnp.concatenate([v, vc], axis=2)
    b, h, _, n, d = q.shape
    nb = n // Q_BLOCK
    q_blocks = jnp.moveaxis(q.reshape(b, h, 2, nb, Q_BLOCK, d), 3, 0)
    y = lax.map(lambda qb: _diff_core(qb, k_all, v_all, lam, scale), q_blocks)
    y = jnp.moveaxis(y, 0, 2).reshape(b, h, n, 2 * d)

    def finish(t):
        return _merge_heads(_rms_norm(t, subln_g) * (1.0 - lambda_init))

    y_ctx = None
    if need_ctx:
        y_ctx = finish(_diff_core(_diff_heads(qc), kc, vc, lam, scale))
    return finish(y), y_ctx

def setup_inputs(seed: int = 0) -> dict:
    key = jax.random.key(seed)
    ks = jax.random.split(key, 13)
    f32 = jnp.float32
    x = jax.random.normal(ks[0], (BATCH, SEQ, D_MODEL), f32)
    c = jax.random.normal(ks[1], (BATCH, D_MODEL), f32)
    ctx = jax.random.normal(ks[2], (BATCH, CTX_LEN, D_MODEL), f32)
    c_ctx = jax.random.normal(ks[3], (D_MODEL,), f32)
    w_mod = jax.random.normal(ks[4], (DEPTH, D_MODEL, 3 * D_MODEL), f32) * (0.5 * D_MODEL ** -0.5)
    b_mod = 0.02 * jax.random.normal(ks[5], (DEPTH, 3 * D_MODEL), f32)
    w_in = jax.random.normal(ks[6], (DEPTH, D_MODEL, 4 * WIDTH), f32) * (D_MODEL ** -0.5)
    w_out = jax.random.normal(ks[7], (DEPTH, WIDTH, D_MODEL), f32) * (WIDTH ** -0.5 * DEEPNORM_BETA)
    ln_g = 1.0 + 0.02 * jax.random.normal(ks[8], (DEPTH, D_MODEL), f32)
    ln_b = 0.02 * jax.random.normal(ks[9], (DEPTH, D_MODEL), f32)
    na_rpb = 0.1 * jax.random.normal(ks[10], (N_NA_LAYERS, NA_HEADS, 2 * NA_WIN_R - 1, 2 * NA_WIN_C - 1), f32)
    diff_lambda = 0.1 * jax.random.normal(ks[11], (N_DIFF_LAYERS, 4, DIFF_HEAD_DIM), f32)
    diff_subln_g = 1.0 + 0.02 * jax.random.normal(ks[12], (N_DIFF_LAYERS, 2 * DIFF_HEAD_DIM), f32)
    return {'x': x, 'c': c, 'ctx': ctx, 'c_ctx': c_ctx, 'w_mod': w_mod, 'b_mod': b_mod,
            'w_in': w_in, 'w_out': w_out, 'ln_g': ln_g, 'ln_b': ln_b, 'na_rpb': na_rpb,
            'diff_lambda': diff_lambda, 'diff_subln_g': diff_subln_g}

def reference(x, c, ctx, c_ctx, w_mod, b_mod, w_in, w_out, ln_g, ln_b, na_rpb, diff_lambda, diff_subln_g):
    cos, sin = _axial_rope_tables(x.shape[1])
    for l in range(DEPTH):
        need_ctx = l < DEPTH - 1
        sh, sc, g = _modulation(c, w_mod[l], b_mod[l])
        sh, sc, g = sh[:, None, :], sc[:, None, :], g[:, None, :]
        shc, scc, gc = _modulation(c_ctx, w_mod[l], b_mod[l])
        h = x * (1.0 + sc) + sh
        hc = ctx * (1.0 + scc) + shc
        q, k, v, z = jnp.split(h @ w_in[l], 4, axis=-1)
        if need_ctx:
            qc, kc, vc, zc = jnp.split(hc @ w_in[l], 4, axis=-1)
        else:
            kc, vc = jnp.split(hc @ w_in[l][:, WIDTH:3 * WIDTH], 2, axis=-1)
            qc, zc = None, None
        if l % N_MIXERS == 0:
            y, yc = _na_mixer(q, k, v, qc, kc, vc, na_rpb[l // N_MIXERS], need_ctx)
        else:
            lambda_init = 0.8 - 0.6 * math.exp(-0.3 * l)
            y, yc = _diff_mixer(q, k, v, qc, kc, vc, diff_lambda[l // N_MIXERS], diff_subln_g[l // N_MIXERS],
                                lambda_init, cos, sin, need_ctx)
        out = (y * jax.nn.silu(z)) @ w_out[l]
        x_new = _layer_norm(DEEPNORM_ALPHA * x + (1.0 + g) * out, ln_g[l], ln_b[l])
        if need_ctx:
            out_c = (yc * jax.nn.silu(zc)) @ w_out[l]
            ctx = _layer_norm(DEEPNORM_ALPHA * ctx + (1.0 + gc) * out_c, ln_g[l], ln_b[l])
        x = x_new
    return x


_drawn_inputs = setup_inputs


def setup_inputs(seed=0):
    import zlib

    import numpy as np

    out = dict(_drawn_inputs(seed))
    spreads = {}
    factors = {'b_mod': 4.179, 'na_rpb': 22.377, 'diff_lambda': 4.286, 'diff_subln_g': 31.224}
    for name, (base, spread) in spreads.items():
        noise = np.random.default_rng([zlib.crc32(name.encode()), seed]).standard_normal(out[name].shape)
        drawn = base * np.exp(spread * noise) if base else spread * noise
        out[name] = jnp.asarray(drawn.astype(out[name].dtype))
    for name, factor in factors.items():
        out[name] = (out[name] * factor).astype(out[name].dtype)
    return out
```

```python
import math
from contextlib import ExitStack

import concourse.bass as bass
import numpy as np
from concourse import mybir

P = 128
D = 1024
SEQ = 1024
CTX = 256
TOK = SEQ + CTX
KT = D // P
NCH = D // P
LAT_TILES, CTX_TILES = SEQ // P, CTX // P
TOK_TILES = LAT_TILES + CTX_TILES
DEPTH = 2
GRID_W = 64
ROWS = SEQ // GRID_W
WIN_R, WIN_C = 8, 16
HEADS = 16
HD = 64
PAD = 63 - (WIN_C - 1)
RPB_W = 2 * WIN_C - 1 + 2 * PAD
RPB_H = 2 * WIN_R - 1
SLOTS = RPB_H - 1
INNER = WIN_R + 1
EPS = 1e-5
ALPHA = (2.0 * DEPTH) ** 0.25
LAMBDA_INIT = 0.8 - 0.6 * math.exp(-0.3 * 1)
SCALE = HD ** -0.5
NEG = -1e30

F32 = mybir.dt.float32
F32R = mybir.dt.float32r
ALU = mybir.AluOpType
ACT = mybir.ActivationFunctionType
AX = mybir.AxisListType.X

GROUPS = [(0, 512), (512, 512), (1024, 256)]
BLOCKS = [2 * D, D, 0, 3 * D]
SWAP16 = [i ^ 16 for i in range(32)]


CREDIT = 1


def f(ap):
    return ap.bitcast(F32)


class Memory:

    def __init__(self, nc, stack):
        def sb(name, shape, dt=F32):
            return stack.enter_context(nc.sbuf_tensor(name, shape, dt))

        self.h_hi = sb("h_hi", [P, KT, TOK], F32R)
        self.h_lo = sb("h_lo", [P, KT, TOK], F32R)
        self.w_raw = sb("w_raw", [P, 2, KT, P])
        self.w_hi = sb("w_hi", [P, 2, KT, P], F32R)
        self.w_lo = sb("w_lo", [P, 2, KT, P], F32R)
        self.q_stack = sb("q_stack", [P, 2, TOK], F32R)
        self.k_dup = sb("k_dup", [P, 2, 2, TOK], F32R)
        self.v = sb("v", [P, TOK_TILES, P])
        self.k_raw = sb("k_raw", [P, TOK])
        self.gate = sb("gate", [P, TOK])
        self.y = sb("y", [P, TOK])
        self.big = sb("big", [P, 5120])
        self.aux = sb("aux", [P, 4608])
        self.pt = sb("pt", [P, 3, 4 * P])
        self.ident = sb("ident", [P, P])
        self.mean_mat = sb("mean_mat", [P, P])
        self.mod_cols = sb("mod_cols", [P, DEPTH, 2, 2 * KT])
        self.b_cols = sb("b_cols", [P, DEPTH, 2 * KT])
        self.cond = sb("cond", [P, 2, KT])
        self.cond_act = sb("cond_act", [P, 2, KT])
        self.neg_lambda = sb("neg_lambda", [P, 1])
        self.sub_gain = sb("sub_gain", [P, 1])
        self.stats = sb("stats", [P, 96])
        self.psum = stack.enter_context(nc.psum_tensor("acc", [P, 8, 512], F32))

    def bank(self, b, width=512):
        return self.psum[:, b, 0:width]

    def banks(self, b, first, last):
        return self.psum[:, :, :].rearrange("p b n -> p (b n)")[:, b * 512 + first:b * 512 + last]


def rows_broadcast(ap_row, n):
    return bass.AP(ap_row.tensor, ap_row.offset, [[0, P], [1, n]])


def modulation(nc, m, stack, w_mod, cond_in, b_cols_in, lam_in, sub_in, ident_in, rpb, toeplitz, gate_rows):
    sem = lambda n: stack.enter_context(nc.semaphore("m_" + n))
    NS = 8
    PIECES = DEPTH * KT * 3
    small_in, lam_loaded, bands = sem("small_in"), sem("lam_loaded"), sem("bands")
    w_in = [sem(f"w_in{s}") for s in range(NS)]
    tanh_done, cond_ready, piece_used = sem("tanh"), sem("cond"), sem("used")
    row_ready, turned, cols_done = sem("row"), sem("turned"), sem("cols")
    gates_out, dve, lam_exp, mean_set = sem("gates_out"), sem("dve"), sem("lam_exp"), sem("mean_set")

    slots = [m.big[:, i * 1024:(i + 1) * 1024] for i in range(4)] + \
            [m.aux[:, i * 1024:(i + 1) * 1024] for i in range(4)]
    row_buf = [b[0:2, i * 512:(i + 1) * 512] for b in (m.k_raw, m.gate, m.y) for i in range(2)]
    lam = m.v[:, 0:2, :].rearrange("p a b -> p (a b)")
    lam_prod = m.v[:, 2, 0:HD]
    sums = m.stats[:, 0:4]

    with nc.Block() as block:
        @block.sync
        def _(sp):
            sp.dma_start(m.cond[:, :, :], cond_in).then_inc(small_in, 16)
            sp.dma_start(m.b_cols[:, :, :], b_cols_in).then_inc(small_in, 16)
            sp.dma_start(m.ident[:, :], ident_in).then_inc(small_in, 16)
            sp.dma_start(lam, rows_broadcast(lam_in, 4 * HD)).then_inc(lam_loaded, 16)
            sp.dma_start(m.sub_gain[:, :], sub_in).then_inc(lam_loaded, 16)
            for n in range(PIECES):
                l, k, j = n // (3 * KT), n // 3 % KT, n % 3
                if n >= NS:
                    sp.wait_ge(piece_used, n - NS + 1)
                sp.dma_start(slots[n % NS], w_mod[l, k * P:(k + 1) * P, j * 1024:(j + 1) * 1024])\
                    .then_inc(w_in[n % NS], 16)
            for l in range(DEPTH):
                sp.wait_ge(row_ready, 6 * (l + 1))
                for j in (4, 5):
                    sp.dma_start(gate_rows[l, :, (j - 4) * 512:(j - 3) * 512], row_buf[j])\
                        .then_inc(gates_out, 16)
            sp.wait_ge(gates_out, 64)

        @block.gpsimd
        def _(pool):
            for h in range(HEADS):
                src = rpb[h, :, 63:127]
                pool.dma_start(toeplitz[h].rearrange("w d j -> d w j"),
                               bass.AP(src.tensor, src.offset, [[RPB_W, RPB_H], [-1, GRID_W], [1, GRID_W]]))\
                    .then_inc(bands, 16)
            pool.wait_ge(bands, 16 * HEADS)

        @block.scalar
        def _(act):
            act.wait_ge(small_in, 48)
            nc.scalar.activation(m.cond_act[:, :, :], m.cond[:, :, :], ACT.Tanh, scale=0.5).then_inc(tanh_done, 1)
            act.wait_ge(dve, 2)
            nc.scalar.activation(sums[:, 2:4], sums[:, 0:2], ACT.Exp).then_inc(lam_exp, 1)

        @block.vector
        def _(v):
            v.wait_ge(tanh_done, 1)
            nc.vector.scalar_tensor_tensor(m.cond_act[:, :, :], m.cond_act[:, :, :], 1.0, m.cond[:, :, :],
                                           ALU.add, ALU.mult).then_inc(cond_ready, 1)
            nc.vector.memset(m.mean_mat[:, :], 1.0 / P).then_inc(mean_set, 1)
            v.wait_ge(lam_loaded, 32)
            for i in range(2):
                if i:
                    v.wait_ge(dve, 1)
                nc.vector.tensor_tensor_reduce(out=lam_prod, in0=lam[:, 2 * i * HD:(2 * i + 1) * HD],
                                               in1=lam[:, (2 * i + 1) * HD:(2 * i + 2) * HD], scale=1.0, scalar=0.0,
                                               op0=ALU.mult, op1=ALU.add, accum_out=sums[:, i:i + 1]).then_inc(dve, 1)
            v.wait_ge(lam_exp, 1)
            nc.vector.tensor_tensor(sums[:, 0:1], sums[:, 3:4], sums[:, 2:3], ALU.subtract).then_inc(dve, 1)
            v.wait_ge(dve, 3)
            nc.vector.tensor_scalar(m.neg_lambda[:, :], sums[:, 0:1], -LAMBDA_INIT, None, ALU.add).then_inc(dve, 1)
            nc.vector.tensor_scalar(m.sub_gain[:, :], m.sub_gain[:, :], 0.5 * (1.0 - LAMBDA_INIT), None, ALU.mult)\
                .then_inc(dve, 1)
            for l in range(DEPTH):
                v.wait_ge(piece_used, 3 * KT * (l + 1))
                if l:
                    v.wait_ge(turned, l)
                    v.wait_ge(gates_out, 32 * l)
                for j in range(6):
                    nc.vector.tensor_scalar(row_buf[j], m.psum[0:2, j, :], 0.5, None, ALU.mult).then_inc(row_ready, 1)
                v.wait_ge(turned, l + 1)
                cols = m.bank(6, 64).rearrange("p (k c) -> p c k", c=2)
                for cnd in range(2):
                    nc.vector.tensor_tensor(m.mod_cols[:, l, cnd, :], cols[:, cnd, 0:2 * KT], m.b_cols[:, l, :], ALU.add)\
                        .then_inc(cols_done, 1)
                    v.wait_ge(cols_done, 4 * l + 2 * cnd + 1)
                    nc.vector.tensor_scalar(m.mod_cols[:, l, cnd, KT:2 * KT], m.mod_cols[:, l, cnd, KT:2 * KT], 1.0,
                                            None, ALU.add).then_inc(cols_done, 1)

        @block.tensor
        def _(pe):
            pe.wait_ge(cond_ready, 1)
            for l in range(DEPTH):
                if l:
                    pe.wait_ge(row_ready, 6 * l)
                for k in range(KT):
                    for j in range(3):
                        n = (l * KT + k) * 3 + j
                        pe.wait_ge(w_in[n % NS], 16 * (n // NS + 1))
                        for half in range(2):
                            mm = nc.tensor.matmul(m.psum[0:2, 2 * j + half, :], m.cond_act[:, :, k],
                                                  slots[n % NS][:, half * 512:(half + 1) * 512],
                                                  start=(k == 0), stop=(k == KT - 1))
                        mm.then_inc(piece_used, 1)
                pe.wait_ge(row_ready, 6 * (l + 1))
                if l:
                    pe.wait_ge(cols_done, 4 * l)
                for k in range(2 * KT):
                    src = row_buf[k // 4][:, (k % 4) * P:(k % 4 + 1) * P]
                    mm = nc.tensor.transpose(m.psum[:, 6, 2 * k:2 * k + 2], src, m.ident[0:2, 0:2])
                mm.then_inc(turned, 1)


def load_tokens(nc, m, stack, l, rows):
    sem = lambda n: stack.enter_context(nc.semaphore(f"t{l}_" + n))
    loaded = [sem(f"loaded{g}") for g in range(3)]
    turned, modulated, hi_done, lo_done = sem("turned"), sem("modulated"), sem("hi"), sem("lo")
    TILES = [range(0, 4), range(4, 8), range(8, 10)]
    buf = [(m.big, m.aux, m.big)[g][:, 0:4096].rearrange("p (t n) -> p t n", t=4) for g in range(3)]
    tmp = [m.k_raw[:, 0:512], m.y[:, 0:512]]
    steps = [(g, k) for g in range(3) for k in range(KT)]

    with nc.Block() as block:
        @block.sync
        def _(sp):
            for g in range(3):
                if g == 2:
                    sp.wait_ge(turned, KT)
                for i, t in enumerate(TILES[g]):
                    sp.dma_start(buf[g][:, i, :], rows(t)).then_inc(loaded[g], 16)

        @block.tensor
        def _(pe):
            for n, (g, k) in enumerate(steps):
                if k == 0:
                    pe.wait_ge(loaded[g], 16 * len(TILES[g]))
                if n >= 4:
                    pe.wait_ge(modulated, n - 3)
                for i in range(len(TILES[g])):
                    mm = nc.tensor.transpose(m.psum[:, n % 4, i * P:(i + 1) * P], buf[g][:, i, k * P:(k + 1) * P],
                                             m.ident[:, :])
                mm.then_inc(turned, 1)

        @block.scalar
        def _(act):
            for n, (g, k) in enumerate(steps):
                w = GROUPS[g][1]
                cnd = g // 2
                act.wait_ge(turned, n + 1)
                if n >= 2:
                    act.wait_ge(lo_done, n - 1)
                nc.scalar.activation(tmp[n % 2][:, 0:w], m.bank(n % 4, w), ACT.Identity,
                                     scale=m.mod_cols[:, l, cnd, KT + k:KT + k + 1],
                                     bias=m.mod_cols[:, l, cnd, k:k + 1]).then_inc(modulated, 1)

        @block.vector
        def _(v):
            for n, (g, k) in enumerate(steps):
                t0, w = GROUPS[g]
                v.wait_ge(modulated, n + 1)
                nc.vector.tensor_copy(m.h_hi[:, k, t0:t0 + w], tmp[n % 2][:, 0:w]).then_inc(hi_done, 1)
                v.wait_ge(hi_done, n + 1)
                nc.vector.tensor_tensor(m.h_lo[:, k, t0:t0 + w], tmp[n % 2][:, 0:w], f(m.h_hi[:, k, t0:t0 + w]),
                                        ALU.subtract).then_inc(lo_done, 1)


class Projection:

    def __init__(self, nc, m, stack, l, w_in, rotary):
        self.counters = []

        def sem(n):
            self.counters.append(stack.enter_context(nc.semaphore(f"p{l}_" + n)))
            return self.counters[-1]

        self.nc, self.m, self.w_in, self.l, self.rotary = nc, m, w_in, l, rotary
        self.w_loaded = [sem("w_loaded0"), sem("w_loaded1")]
        self.w_hi, self.w_split, self.proj = sem("w_hi"), sem("w_split"), sem("proj")
        self.evac, self.gate_done = sem("evac"), sem("gate_done")
        self.tanh_done = sem("tanh")
        self.v_turned, self.v_ready = sem("v_turned"), sem("v_ready")
        self.k_own, self.k_ready, self.q_ready = sem("k_own"), sem("k_ready"), sem("q_ready")
        self.rot_shuffled, self.rot_scaled, self.dve = sem("rot_shuffled"), sem("rot_scaled"), sem("rot_dve")
        self.split_hi = sem("split_hi")
        lat_only = l == DEPTH - 1
        self.q_groups = 2 if lat_only else 3
        self.q_cols = SEQ if lat_only else TOK
        sizes = [3, 3, self.q_groups, self.q_groups]
        self.cum = [sum(sizes[:b + 1]) for b in range(4)]
        self.G = self.cum[-1]
        self.groups = [(b, g) for b in range(4) for g in range(sizes[b])]

    def give_credit(self, sp, counters):
        for s in self.counters + counters:
            sp.sem_inc(s, CREDIT)

    def load(self, sp, c, b):
        col = BLOCKS[b % 4] + (c + b // 4) * P
        src = self.w_in[self.l].rearrange("(k p) n -> p k n", p=P)[:, :, bass.ds(col, P)]
        sp.dma_start(self.m.w_raw[:, b % 2, :, :], src).then_inc(self.w_loaded[b % 2], 16)

    def load_next(self, sp, c):
        for b in (2, 3, 4, 5):
            sp.wait_ge(self.w_split, CREDIT + c * 4 + (b - 1))
            self.load(sp, c, b)

    def split_hi_part(self, act, c, b):
        act.wait_ge(self.w_loaded[b % 2], CREDIT + c * 32 + 16 * (b // 2 + 1))
        if b >= 1:
            act.wait_ge(self.proj, CREDIT + c * self.G + ([0] + self.cum)[b - 1])
        self.nc.scalar.activation(self.m.w_hi[:, b % 2, :, :], self.m.w_raw[:, b % 2, :, :], ACT.Copy)\
            .then_inc(self.w_hi, 1)

    def split_lo_part(self, v, c, b):
        v.wait_ge(self.w_hi, CREDIT + c * 4 + (b + 1))
        self.nc.vector.tensor_tensor(self.m.w_lo[:, b % 2, :, :], self.m.w_raw[:, b % 2, :, :],
                                     f(self.m.w_hi[:, b % 2, :, :]), ALU.subtract).then_inc(self.w_split, 1)

    def evac_before(self, j):
        last = j - 4
        return last + 1 if last < self.cum[2] else None

    def products(self, pe, c, b, s_free):
        nc, m = self.nc, self.m
        pe.wait_ge(self.w_split, CREDIT + c * 4 + (b + 1))
        for j, (bb, g) in enumerate(self.groups):
            if bb != b:
                continue
            t0, w = GROUPS[g]
            if j == 0:
                s_free(pe)
            if j >= 4:
                pe.wait_ge(self.evac, CREDIT + c * self.cum[2] + (j - 3))
            for k in range(KT):
                for i, (wt, ht) in enumerate(((m.w_hi, m.h_hi), (m.w_hi, m.h_lo), (m.w_lo, m.h_hi))):
                    mm = nc.tensor.matmul(m.bank(j % 4, w), wt[:, b % 2, k, :], ht[:, k, t0:t0 + w],
                                          start=(k == 0 and i == 0), stop=(k == KT - 1 and i == 2))
            mm.then_inc(self.proj, 1)

    def turn_v(self, pe, c, t_free):
        t_free(pe)
        pe.wait_ge(self.evac, CREDIT + c * self.cum[2] + 3)
        for g, (t0, w) in enumerate(GROUPS):
            if g == 2:
                pe.wait_ge(self.v_ready, CREDIT + c * 3 + 1)
            for i in range(w // P):
                mm = self.nc.tensor.transpose(self.m.psum[:, 4 + g % 2, i * P:(i + 1) * P],
                                              self.m.gate[:, t0 + i * P:t0 + (i + 1) * P], self.m.ident[:, :])
            mm.then_inc(self.v_turned, 1)

    def evacuate(self, act, c, b):
        dst = (self.m.gate, self.m.k_raw, self.m.y)[b]
        for j, (bb, g) in enumerate(self.groups):
            if bb != b:
                continue
            t0, w = GROUPS[g]
            act.wait_ge(self.proj, CREDIT + c * self.G + (j + 1))
            self.nc.scalar.activation(dst[:, t0:t0 + w], self.m.bank(j % 4, w), ACT.Copy,
                                      scale=SCALE if b == 2 else 1.0).then_inc(self.evac, 1)

    def evacuate_v(self, act, c):
        for g, (t0, w) in enumerate(GROUPS):
            act.wait_ge(self.v_turned, CREDIT + c * 3 + (g + 1))
            self.nc.scalar.activation(self.m.v[:, t0 // P:(t0 + w) // P, :],
                                      self.m.bank(4 + g % 2, w).rearrange("p (t n) -> p t n", n=P), ACT.Copy)\
                .then_inc(self.v_ready, 1)

    def duplicate_k(self, act, c):
        act.wait_ge(self.k_own, CREDIT + c * 2 + 2)
        for h in range(2):
            own, other = slice(64 * h, 64 * h + 64), slice(64 - 64 * h, 128 - 64 * h)
            self.nc.scalar.activation(self.m.k_dup[other, h, :, :], f(self.m.k_dup[own, h, :, :]), ACT.Copy)\
                .then_inc(self.k_ready, 1)

    def gate_tanh(self, act, c):
        act.wait_ge(self.v_ready, CREDIT + c * 3 + 3)
        for j, (b, g) in enumerate(self.groups):
            if b == 3:
                t0, w = GROUPS[g]
                act.wait_ge(self.proj, CREDIT + c * self.G + (j + 1))
                self.nc.scalar.activation(self.m.gate[:, t0:t0 + w], self.m.bank(j % 4, w), ACT.Tanh, scale=0.5)\
                    .then_inc(self.tanh_done, 1)

    def gate_silu(self, v, c):
        for j, (b, g) in enumerate(self.groups):
            if b == 3:
                t0, w = GROUPS[g]
                v.wait_ge(self.tanh_done, CREDIT + c * self.q_groups + (g + 1))
                self.nc.vector.scalar_tensor_tensor(self.m.gate[:, t0:t0 + w], self.m.gate[:, t0:t0 + w], 1.0,
                                                    self.m.bank(j % 4, w), ALU.add, ALU.mult)\
                    .then_inc(self.gate_done, 1)

    def rotate(self, v, c, x, turn):
        rot, scaled = self.m.big[:, 0:SEQ], self.m.big[:, SEQ:2 * SEQ]
        self.nc.vector.tensor_tensor(scaled, x[:, 0:SEQ], self.m.aux[:, 0:SEQ], ALU.mult).then_inc(self.dve, 1)
        self.nc.vector.stream_shuffle(rot, x[:, 0:SEQ], SWAP16).then_inc(self.rot_shuffled, 1)
        v.wait_ge(self.dve, CREDIT + c * 4 + (2 * turn + 1))
        v.wait_ge(self.rot_scaled, CREDIT + c * 2 + (turn + 1))
        self.nc.vector.tensor_tensor(x[:, 0:SEQ], scaled, rot, ALU.add).then_inc(self.dve, 1)
        v.wait_ge(self.dve, CREDIT + c * 4 + (2 * turn + 2))

    def scale_partner(self, pool, c):
        for turn in range(2):
            pool.wait_ge(self.rot_shuffled, CREDIT + c * 2 + (turn + 1))
            self.nc.gpsimd.tensor_tensor(self.m.big[:, 0:SEQ], self.m.big[:, 0:SEQ], self.m.aux[:, SEQ:2 * SEQ],
                                         ALU.mult).then_inc(self.rot_scaled, 1)

    def split_k(self, v, c):
        v.wait_ge(self.evac, CREDIT + c * self.cum[2] + self.cum[1])
        if self.rotary:
            self.rotate(v, c, self.m.k_raw, 0)
        m = self.m
        for h in range(2):
            own = slice(64 * h, 64 * h + 64)
            self.nc.vector.tensor_copy(m.k_dup[own, h, 0, :], m.k_raw[own, :]).then_inc(self.split_hi, 1)
        for h in range(2):
            own = slice(64 * h, 64 * h + 64)
            v.wait_ge(self.split_hi, CREDIT + c * 4 + (h + 1))
            self.nc.vector.tensor_tensor(m.k_dup[own, h, 1, :], m.k_raw[own, :], f(m.k_dup[own, h, 0, :]),
                                         ALU.subtract).then_inc(self.k_own, 1)

    def split_q(self, v, c):
        v.wait_ge(self.evac, CREDIT + c * self.cum[2] + self.cum[2])
        if self.rotary:
            self.rotate(v, c, self.m.y, 1)
        m, n = self.m, self.q_cols
        for h in range(2):
            own = slice(64 * h, 64 * h + 64)
            self.nc.vector.tensor_copy(m.q_stack[own, h, 0:n], m.y[own, 0:n]).then_inc(self.split_hi, 1)
        for h in range(2):
            own, other = slice(64 * h, 64 * h + 64), slice(64 - 64 * h, 128 - 64 * h)
            v.wait_ge(self.split_hi, CREDIT + c * 4 + (h + 3))
            self.nc.vector.tensor_tensor(m.q_stack[other, h, 0:n], m.y[own, 0:n], f(m.q_stack[own, h, 0:n]),
                                         ALU.subtract).then_inc(self.q_ready, 1)

    def act_part(self, act, c, gate_free, y_free):
        self.split_hi_part(act, c, 1)
        gate_free(act)
        self.evacuate(act, c, 0)
        self.split_hi_part(act, c, 2)
        self.evacuate(act, c, 1)
        self.split_hi_part(act, c, 3)
        self.evacuate_v(act, c)
        y_free(act)
        self.evacuate(act, c, 2)
        self.duplicate_k(act, c)
        self.split_hi_part(act, c, 4)
        self.gate_tanh(act, c)

    def dve_part(self, v, c):
        for b in (1, 2, 3):
            self.split_lo_part(v, c, b)
        self.split_k(v, c)
        self.split_q(v, c)
        self.split_lo_part(v, c, 4)
        self.gate_silu(v, c)

    def pe_part(self, pe, c, s_free, t_free):
        self.products(pe, c, 0, s_free)
        self.products(pe, c, 1, s_free)
        self.turn_v(pe, c, t_free)
        self.products(pe, c, 2, s_free)
        self.products(pe, c, 3, s_free)
        pe.wait_ge(self.q_ready, CREDIT + c * 2 + 2)
        pe.wait_ge(self.k_ready, CREDIT + c * 2 + 2)
        pe.wait_ge(self.gate_done, CREDIT + c * self.q_groups + self.q_groups)


class Item:

    def __init__(self, head, qt):
        self.head, self.qt = head, qt
        self.local = qt < LAT_TILES
        self.rows = 0
        if self.local:
            r = 2 * qt
            start = [min(max(x - WIN_R // 2, 0), ROWS - WIN_R) for x in (r, r + 1)]
            self.k0 = start[0]
            self.rows = start[1] + WIN_R - start[0]
            self.slot = self.k0 - r + WIN_R - 2
        self.width = CTX + self.rows * GRID_W
        tiles = [LAT_TILES + i for i in range(CTX_TILES)]
        if self.local:
            tiles += [self.k0 // 2 + i for i in range((self.rows + 1) // 2)]
        self.key_tiles = tiles
        self.y_group = head * 3 + qt // 4


def neighbourhood(nc, m, stack, w_in, toeplitz, masks_in, y_out):
    l = 0
    p = Projection(nc, m, stack, l, w_in, rotary=False)
    counters = []

    def sem(n):
        counters.append(stack.enter_context(nc.semaphore("n_" + n)))
        return counters[-1]

    masks_loaded = stack.enter_context(nc.semaphore("n_masks"))
    bias_loaded, bias_ready, bias_tmp = sem("bias_loaded"), sem("bias_ready"), sem("bias_tmp")
    s_done, raw_max, max_done = sem("s_done"), sem("raw_max"), sem("max_done")
    exp_done, recip_done, p_ready = sem("exp_done"), sem("recip"), sem("p_ready")
    turned, pt_ready, av_done, y_ready, y_stored = sem("turned"), sem("pt_ready"), sem("av_done"), sem("y_ready"), sem("y_stored")
    pad_set = stack.enter_context(nc.semaphore("n_pad"))

    items = [Item(h, qt) for h in range(2) for qt in range(TOK_TILES)]
    NI = len(items)
    NL = sum(it.local for it in items)
    WMAX = CTX + (INNER + 1) * GRID_W
    PB = 4
    prob = m.big[:, 0:PB * WMAX].rearrange("p (b n) -> p b n", b=PB)
    mask_w = SLOTS * GRID_W
    inner_w = INNER * GRID_W
    mask = m.aux[:, 0:mask_w + inner_w]
    mask_all, mask_inner = mask[:, 0:mask_w], mask[:, mask_w:]
    bias = m.aux[:, 1536:1536 + 2 * mask_w].rearrange("p (h n) -> p h n", h=2)
    bias_inner = m.aux[:, 1536 + 2 * mask_w:1536 + 2 * (mask_w + inner_w)].rearrange("p (h n) -> p h n", h=2)
    turns = [(i, a, min(4, len(it.key_tiles) - a)) for i, it in enumerate(items) for a in range(0, len(it.key_tiles), 4)]
    of_item = [[n for n, t in enumerate(turns) if t[0] == i] for i in range(NI)]
    NT = len(turns)
    YG = 6
    last_item = [max(i for i, it in enumerate(items) if it.y_group == g) for g in range(YG)]
    local_before = [sum(x.local for x in items[:i]) for i in range(NI + 1)]
    assert NI % 2 == 0 and NT % 6 == 0 and NI % PB == 0

    def stat(i, col):
        return m.stats[:, (i % 4) * 8 + col:(i % 4) * 8 + col + 1]

    with nc.Block() as block:
        @block.sync
        def _(sp):
            p.give_credit(sp, counters)
            sp.dma_start(mask, masks_in).then_inc(masks_loaded, 16)
            p.load(sp, 0, 0)
            p.load(sp, 0, 1)
            with sp.Fori(0, NCH) as c:
                sp.wait_ge(max_done, CREDIT + c * NI)
                for half in range(2):
                    src = toeplitz[bass.ds(c * 2, 2), :, 1 - half:1 - half + SLOTS, :].rearrange("h w d j -> w h (d j)")
                    sp.dma_start(bias[64 * half:64 * half + 64, :, :], src).then_inc(bias_loaded, 16)
                p.load_next(sp, c)
                sp.wait_ge(y_ready, CREDIT + c * YG + YG)
                sp.dma_start(y_out[bass.ds(c * P, P), :], m.y[:, :]).then_inc(y_stored, 16)
            sp.wait_ge(y_stored, CREDIT + 16 * NCH)

        @block.gpsimd
        def _(pool):
            nc.gpsimd.memset(prob[:, :, WMAX - GRID_W:WMAX], 0.0).then_inc(pad_set, 1)
            pool.wait_ge(masks_loaded, 16)
            with pool.Fori(0, NCH) as c:
                pool.wait_ge(bias_loaded, CREDIT + c * 32 + 32)
                for h in range(2):
                    nc.gpsimd.tensor_tensor(bias_inner[:, h, :], bias[:, h, 2 * GRID_W:2 * GRID_W + inner_w], mask_inner,
                                            ALU.add).then_inc(bias_tmp, 1)
                for h in range(2):
                    pool.wait_ge(bias_tmp, CREDIT + c * 2 + (h + 1))
                    nc.gpsimd.tensor_tensor(bias[:, h, :], bias[:, h, :], mask_all, ALU.add).then_inc(bias_ready, 1)

        @block.scalar
        def _(act):
            p.split_hi_part(act, 0, 0)
            act.wait_ge(pad_set, 1)

            with act.Fori(0, NCH) as c:
                def exp(i):
                    it = items[i]
                    act.wait_ge(max_done, CREDIT + c * NI + (i + 1))
                    nc.scalar.activation(prob[:, i % PB, 0:it.width], m.banks(2 * (i % 2), 0, it.width), ACT.Exp,
                                         bias=stat(i, 2), accum_out=stat(i, 3)).then_inc(exp_done, 1)

                def evac(n):
                    w = turns[n][2] * P
                    act.wait_ge(turned, CREDIT + c * NT + (n + 1))
                    act.wait_ge(av_done, CREDIT + c * NT + max(n - 2, 0))
                    nc.scalar.activation(m.pt[:, n % 3, 0:w], m.bank(4 + n % 2, w), ACT.Copy).then_inc(pt_ready, 1)

                p.act_part(act, c, lambda e: e.wait_ge(y_ready, CREDIT + c * YG), lambda e: e.wait_ge(y_stored, CREDIT + c * 16))
                exp(0)
                for i in range(NI):
                    if i + 1 < NI:
                        exp(i + 1)
                    for n in of_item[i]:
                        evac(n)

        @block.vector
        def _(v):
            p.split_lo_part(v, 0, 0)

            with v.Fori(0, NCH) as c:
                def row_max(i):
                    it = items[i]
                    s = 2 * (i % 2)
                    v.wait_ge(s_done, CREDIT + c * NI + (i + 1))
                    if not it.local:
                        nc.vector.reduce_max(stat(i, 2), m.banks(s, 0, CTX), AX, negate=True).then_inc(max_done, 1)
                        return
                    nl = local_before[i]
                    nc.vector.reduce_max(stat(i, 0), m.banks(s, 0, CTX), AX)
                    if it.rows == INNER:
                        b = bias_inner[:, it.head, :]
                    else:
                        b = bias[:, it.head, it.slot * GRID_W:(it.slot + WIN_R) * GRID_W]
                    loc = m.banks(s, CTX, it.width)
                    nc.vector.tensor_tensor_reduce(out=loc, in0=loc, in1=b, scale=1.0, scalar=-3e38, op0=ALU.add,
                                                   op1=ALU.max, accum_out=stat(i, 1)).then_inc(raw_max, 1)
                    v.wait_ge(raw_max, CREDIT + c * NL + (nl + 1))
                    nc.vector.reduce_max(stat(i, 2), m.stats[:, (i % 4) * 8:(i % 4) * 8 + 2], AX, negate=True)\
                        .then_inc(max_done, 1)

                def normalise(i):
                    it = items[i]
                    v.wait_ge(exp_done, CREDIT + c * NI + (i + 1))
                    nc.vector.reciprocal(stat(i, 4), stat(i, 3)).then_inc(recip_done, 1)
                    v.wait_ge(recip_done, CREDIT + c * NI + (i + 1))
                    pr = prob[:, i % PB, 0:it.width]
                    nc.vector.tensor_scalar(pr, pr, stat(i, 4), None, ALU.mult).then_inc(p_ready, 1)

                def gate_y(g):
                    h, t0 = g // 3, (g % 3) * 512
                    w = min(512, TOK - t0)
                    own = slice(64 * h, 64 * h + 64)
                    v.wait_ge(av_done, CREDIT + c * NT + (of_item[last_item[g]][-1] + 1))
                    nc.vector.scalar_tensor_tensor(m.y[own, t0:t0 + w], m.psum[own, 6 + g % 2, 0:w], 0.5,
                                                   m.gate[own, t0:t0 + w], ALU.mult, ALU.mult).then_inc(y_ready, 1)

                p.dve_part(v, c)
                v.wait_ge(bias_ready, CREDIT + c * 2 + 2)
                row_max(0)
                row_max(1)
                for i in range(NI):
                    normalise(i)
                    if i + 2 < NI:
                        row_max(i + 2)
                    if i - 2 in last_item:
                        gate_y(last_item.index(i - 2))
                for g in range(YG):
                    if last_item[g] + 2 >= NI:
                        gate_y(g)

        @block.tensor
        def _(pe):
            with pe.Fori(0, NCH) as c:
                def scores(i):
                    it = items[i]
                    s = 2 * (i % 2)
                    if i >= 2:
                        pe.wait_ge(exp_done, CREDIT + c * NI + (i - 1))
                    parts = [(s, 0, CTX, SEQ)]
                    if it.local:
                        k0 = it.k0 * GRID_W
                        parts += [(s, CTX, 256, k0), (s + 1, 0, (it.rows - 4) * GRID_W, k0 + 256)]
                    for b, col, w, key in parts:
                        for part in range(2):
                            mm = nc.tensor.matmul(m.psum[:, b, col:col + w], m.q_stack[:, it.head, it.qt * P:(it.qt + 1) * P],
                                                  m.k_dup[:, it.head, part, key:key + w], start=(part == 0), stop=(part == 1))
                    mm.then_inc(s_done, 1)

                def turn(n):
                    i, a, cnt = turns[n]
                    pe.wait_ge(p_ready, CREDIT + c * NI + (i + 1))
                    if n >= 2:
                        pe.wait_ge(pt_ready, CREDIT + c * NT + (n - 1))
                    for t in range(cnt):
                        mm = nc.tensor.transpose(m.psum[:, 4 + n % 2, t * P:(t + 1) * P],
                                                 prob[:, i % PB, (a + t) * P:(a + t + 1) * P], m.ident[:, :])
                    mm.then_inc(turned, 1)

                def values(n):
                    i, a, cnt = turns[n]
                    it = items[i]
                    pe.wait_ge(pt_ready, CREDIT + c * NT + (n + 1))
                    if a == 0 and it.qt % 4 == 0:
                        pe.wait_ge(y_ready, CREDIT + c * YG + max(it.y_group - 1, 0))
                    for t in range(cnt):
                        mm = nc.tensor.matmul(m.psum[:, 6 + it.y_group % 2, (it.qt % 4) * P:(it.qt % 4 + 1) * P],
                                              m.v[:, it.key_tiles[a + t], :], m.pt[:, n % 3, t * P:(t + 1) * P],
                                              start=(a + t == 0), stop=(a + t == len(it.key_tiles) - 1))
                    mm.then_inc(av_done, 1)

                p.pe_part(pe, c, lambda e: e.wait_ge(exp_done, CREDIT + c * NI), lambda e: e.wait_ge(pt_ready, CREDIT + c * NT))
                pe.wait_ge(p.v_ready, CREDIT + c * 3 + 3)
                scores(0)
                scores(1)
                for i in range(NI + 1):
                    if i + 2 < NI:
                        scores(i + 2)
                    new = of_item[i] if i < NI else []
                    old = of_item[i - 1] if i else []
                    for n in range(2):
                        if n < len(new):
                            turn(new[n])
                        if n < len(old):
                            values(old[n])


def differential(nc, m, stack, w_in, rope_in, y_out):
    l = 1
    p = Projection(nc, m, stack, l, w_in, rotary=True)
    counters = []

    def sem(n):
        counters.append(stack.enter_context(nc.semaphore("d_" + n)))
        return counters[-1]

    rope_loaded = stack.enter_context(nc.semaphore("d_rope"))
    s_done, max_done, exp_done, coef, p_ready = sem("s_done"), sem("max_done"), sem("exp_done"), sem("coef"), sem("p_ready")
    turned, pt_ready, av_done = sem("turned"), sem("pt_ready"), sem("av_done")
    y_raw, sq_done, sq_ready, ms_done, root_done = sem("y_raw"), sem("sq_done"), sem("sq_ready"), sem("ms_done"), sem("root_done")
    y_ready, y_stored, fin = sem("y_ready"), sem("y_stored"), sem("fin")

    NQ = LAT_TILES
    KEYS = TOK_TILES
    turns = [(t, a, min(4, KEYS - a)) for t in range(NQ) for a in range(0, KEYS, 4)]
    TPT = 3
    NT = len(turns)
    prob = m.big[:, 0:4 * TOK].rearrange("p (b n) -> p b n", b=4)
    y_sb, sq = m.aux[:, 2048:3072], m.aux[:, 3072:4096]
    stat = lambda t, col: m.stats[:, (t % 2) * 8 + col:(t % 2) * 8 + col + 1]
    eps_col = lambda t: m.stats[:, 32 + t:33 + t]

    with nc.Block() as block:
        @block.sync
        def _(sp):
            p.give_credit(sp, counters)
            sp.dma_start(m.aux[:, 0:2 * SEQ].rearrange("p (a n) -> p a n", a=2), rope_in).then_inc(rope_loaded, 16)
            p.load(sp, 0, 0)
            p.load(sp, 0, 1)
            with sp.Fori(0, NCH) as c:
                p.load_next(sp, c)
                sp.wait_ge(y_ready, CREDIT + c * 2 + 2)
                sp.dma_start(y_out[bass.ds(c * P, P), 0:SEQ], m.y[:, 0:SEQ]).then_inc(y_stored, 16)
            sp.wait_ge(y_stored, CREDIT + 16 * NCH)

        @block.gpsimd
        def _(pool):
            pool.wait_ge(rope_loaded, 16)
            with pool.Fori(0, NCH) as c:
                p.scale_partner(pool, c)

        @block.scalar
        def _(act):
            p.split_hi_part(act, 0, 0)

            with act.Fori(0, NCH) as c:
                def exp(mp, t):
                    act.wait_ge(max_done, CREDIT + c * 2 * NQ + (2 * t + mp + 1))
                    nc.scalar.activation(prob[:, 2 * (t % 2) + mp, :], m.banks(3 * mp, 0, TOK), ACT.Exp,
                                         bias=stat(t, mp), accum_out=stat(t, 2 + mp)).then_inc(exp_done, 1)

                def evac(n):
                    w = turns[n][2] * P
                    act.wait_ge(turned, CREDIT + c * NT + (n + 1))
                    act.wait_ge(av_done, CREDIT + c * NT + max(n - 2, 0))
                    nc.scalar.activation(m.pt[:, n % 3, 0:w], m.bank(6, w), ACT.Copy).then_inc(pt_ready, 1)

                def take_y(half):
                    cols = slice(half * 512, half * 512 + 512)
                    act.wait_ge(av_done, CREDIT + c * NT + 4 * TPT * (half + 1))
                    nc.scalar.activation(y_sb[:, cols], m.bank(7), ACT.Copy).then_inc(y_raw, 1)
                    act.wait_ge(y_raw, CREDIT + c * 2 + (half + 1))
                    nc.scalar.activation(sq[:, cols], y_sb[:, cols], ACT.Square).then_inc(sq_done, 1)

                p.act_part(act, c, lambda e: e.wait_ge(y_ready, CREDIT + c * 2), lambda e: e.wait_ge(y_stored, CREDIT + c * 16))
                exp(0, 0)
                exp(1, 0)
                for t in range(NQ):
                    if t == 4:
                        take_y(0)
                    evac(TPT * t)
                    if t + 1 < NQ:
                        exp(0, t + 1)
                    evac(TPT * t + 1)
                    if t + 1 < NQ:
                        exp(1, t + 1)
                    evac(TPT * t + 2)
                take_y(1)
                for half in range(2):
                    act.wait_ge(ms_done, CREDIT + c * 2 + (half + 1))
                    nc.scalar.activation(sq[:, half * 512:half * 512 + 512], m.bank(4 + half), ACT.Sqrt)\
                        .then_inc(root_done, 1)

        @block.vector
        def _(v):
            p.split_lo_part(v, 0, 0)
            v.wait_ge(rope_loaded, 16)

            with v.Fori(0, NCH) as c:
                def row_max(mp, t):
                    v.wait_ge(s_done, CREDIT + c * 2 * NQ + (2 * t + mp + 1))
                    nc.vector.reduce_max(stat(t, mp), m.banks(3 * mp, 0, TOK), AX, negate=True).then_inc(max_done, 1)

                def combine(t):
                    v.wait_ge(exp_done, CREDIT + c * 2 * NQ + (2 * t + 2))
                    nc.vector.reciprocal(stat(t, 4), stat(t, 3)).then_inc(coef, 1)
                    nc.vector.tensor_scalar(eps_col(t), stat(t, 2), stat(t, 2), EPS * P, ALU.mult, ALU.mult).then_inc(coef, 1)
                    v.wait_ge(coef, CREDIT + c * 3 * NQ + (3 * t + 2))
                    nc.vector.tensor_scalar(stat(t, 5), stat(t, 2), stat(t, 4), m.neg_lambda[:, :], ALU.mult, ALU.mult)\
                        .then_inc(coef, 1)
                    v.wait_ge(coef, CREDIT + c * 3 * NQ + (3 * t + 3))
                    e0, e1 = prob[:, 2 * (t % 2), :], prob[:, 2 * (t % 2) + 1, :]
                    nc.vector.scalar_tensor_tensor(e0, e1, stat(t, 5), e0, ALU.mult, ALU.add).then_inc(p_ready, 1)

                def add_eps(half):
                    v.wait_ge(sq_done, CREDIT + c * 2 + (half + 1))
                    for t in range(4 * half, 4 * half + 4):
                        s = sq[:, t * P:(t + 1) * P]
                        nc.vector.scalar_tensor_tensor(s, m.ident[:, :], eps_col(t), s, ALU.mult, ALU.add).then_inc(sq_ready, 1)

                def finish(half):
                    cols = slice(half * 512, half * 512 + 512)
                    v.wait_ge(root_done, CREDIT + c * 2 + (half + 1))
                    nc.vector.reciprocal(sq[:, cols], sq[:, cols]).then_inc(fin, 1)
                    v.wait_ge(fin, CREDIT + c * 4 + (2 * half + 1))
                    nc.vector.scalar_tensor_tensor(y_sb[:, cols], y_sb[:, cols], m.sub_gain[:, :], sq[:, cols],
                                                   ALU.mult, ALU.mult).then_inc(fin, 1)
                    v.wait_ge(fin, CREDIT + c * 4 + (2 * half + 2))
                    nc.vector.tensor_tensor(m.y[:, cols], y_sb[:, cols], m.gate[:, cols], ALU.mult).then_inc(y_ready, 1)

                p.dve_part(v, c)
                row_max(0, 0)
                row_max(1, 0)
                combine(0)
                for t in range(1, NQ):
                    row_max(0, t)
                    row_max(1, t)
                    combine(t)
                    if t == 5:
                        add_eps(0)
                add_eps(1)
                finish(0)
                finish(1)

        @block.tensor
        def _(pe):
            with pe.Fori(0, NCH) as c:
                def scores(mp, t):
                    if t:
                        pe.wait_ge(exp_done, CREDIT + c * 2 * NQ + (2 * (t - 1) + mp + 1))
                    for g, (k0, w) in enumerate(GROUPS):
                        for part in range(2):
                            mm = nc.tensor.matmul(m.bank(3 * mp + g, w), m.q_stack[:, mp, t * P:(t + 1) * P],
                                                  m.k_dup[:, mp, part, k0:k0 + w], start=(part == 0), stop=(part == 1))
                    mm.then_inc(s_done, 1)

                def turn(n):
                    t, a, cnt = turns[n]
                    pe.wait_ge(p_ready, CREDIT + c * NQ + (t + 1))
                    pe.wait_ge(pt_ready, CREDIT + c * NT + n)
                    for i in range(cnt):
                        mm = nc.tensor.transpose(m.psum[:, 6, i * P:(i + 1) * P],
                                                 prob[:, 2 * (t % 2), (a + i) * P:(a + i + 1) * P], m.ident[:, :])
                    mm.then_inc(turned, 1)

                def values(n):
                    t, a, cnt = turns[n]
                    pe.wait_ge(pt_ready, CREDIT + c * NT + (n + 1))
                    if a == 0 and t % 4 == 0:
                        pe.wait_ge(y_raw, CREDIT + c * 2 + t // 4)
                    for i in range(cnt):
                        mm = nc.tensor.matmul(m.psum[:, 7, (t % 4) * P:(t % 4 + 1) * P], m.v[:, a + i, :],
                                              m.pt[:, n % 3, i * P:(i + 1) * P], start=(a + i == 0), stop=(a + i == KEYS - 1))
                    mm.then_inc(av_done, 1)

                p.pe_part(pe, c, lambda e: e.wait_ge(exp_done, CREDIT + c * 2 * NQ), lambda e: e.wait_ge(root_done, CREDIT + c * 2))
                pe.wait_ge(p.v_ready, CREDIT + c * 3 + 3)
                scores(0, 0)
                scores(1, 0)
                for t in range(NQ):
                    if t + 1 < NQ:
                        scores(0, t + 1)
                    if t:
                        values(TPT * t - 1)
                    turn(TPT * t)
                    if t + 1 < NQ:
                        scores(1, t + 1)
                    turn(TPT * t + 1)
                    values(TPT * t)
                    turn(TPT * t + 2)
                    values(TPT * t + 1)
                values(NT - 1)
                pe.wait_ge(exp_done, CREDIT + c * 2 * NQ + 2 * NQ)
                for half in range(2):
                    pe.wait_ge(sq_ready, CREDIT + c * NQ + 4 * (half + 1))
                    nc.tensor.matmul(m.bank(4 + half), m.mean_mat[:, :], sq[:, half * 512:half * 512 + 512],
                                     start=True, stop=True).then_inc(ms_done, 1)


def project(nc, m, stack, l, w_out, y_in, gate_rows, b_gate, ln_g, ln_b, rows, out_rows, tiles):
    sem = lambda n: stack.enter_context(nc.semaphore(f"o{l}_" + n))
    w_loaded, y_loaded, x_loaded = ([sem(f"{n}{s}") for s in range(2)] for n in ("w", "y", "x"))
    stored = [sem(f"stored{s}") for s in range(2)]
    w_hi, w_ready, y_hi, y_ready, mm_done = sem("w_hi"), sem("w_ready"), sem("y_hi"), sem("y_ready"), sem("mm_done")
    rows_in, gains, dve, psum_free, x_free = sem("rows_in"), sem("gains"), sem("dve"), sem("psum_free"), sem("x_free")
    var_done, root_done, normed = sem("var"), sem("root"), sem("normed")

    stage = [m.k_raw[:, 0:D], m.gate[:, 0:D]]
    x_buf = [m.big[:, s * D:(s + 1) * D] for s in range(2)]
    t_buf = [m.big[:, (2 + s) * D:(3 + s) * D] for s in range(2)]
    b_row = m.big[:, 4 * D:5 * D]
    gain = [m.aux[:, s * D:(s + 1) * D] for s in range(2)]
    g_row, beta_row = m.aux[:, 2 * D:3 * D], m.aux[:, 3 * D:4 * D]
    conds = 2 if tiles > LAT_TILES else 1

    def stat(i, a, b):
        return m.stats[:, (i % 2) * 24 + a:(i % 2) * 24 + b]

    with nc.Block() as block:
        @block.sync
        def _(sp):
            for cnd in range(conds):
                sp.dma_start(gain[cnd], rows_broadcast(gate_rows[l, cnd, :], D)).then_inc(rows_in, 16)
            sp.dma_start(b_row, rows_broadcast(b_gate[l, :], D)).then_inc(rows_in, 16)
            sp.dma_start(g_row, rows_broadcast(ln_g[l, :], D)).then_inc(rows_in, 16)
            sp.dma_start(beta_row, rows_broadcast(ln_b[l, :], D)).then_inc(rows_in, 16)
            for k in range(KT):
                if k >= 2:
                    sp.wait_ge(w_ready, k - 1)
                sp.dma_start(stage[k % 2], w_out[l, k * P:(k + 1) * P, :]).then_inc(w_loaded[k % 2], 16)

        @block.gpsimd
        def _(pool):
            for i in range(tiles):
                if i >= 2:
                    pool.wait_ge(y_ready, i - 1)
                pool.dma_start(m.w_raw[:, i % 2, :, :],
                               y_in.rearrange("(k p) n -> p k n", p=P)[:, :, i * P:(i + 1) * P])\
                    .then_inc(y_loaded[i % 2], 16)
                if i >= 2:
                    pool.wait_ge(x_free, i - 1)
                pool.dma_start(x_buf[i % 2], rows(i)).then_inc(x_loaded[i % 2], 16)

        @block.scalar
        def _(act):
            def split_y(i):
                act.wait_ge(y_loaded[i % 2], 16 * (i // 2 + 1))
                if i >= 2:
                    act.wait_ge(mm_done, i - 1)
                nc.scalar.activation(m.w_hi[:, i % 2, :, :], m.w_raw[:, i % 2, :, :], ACT.Copy).then_inc(y_hi, 1)

            split_y(0)
            for k in range(KT):
                act.wait_ge(w_loaded[k % 2], 16 * (k // 2 + 1))
                nc.scalar.activation(m.h_hi[:, k, 0:D], stage[k % 2], ACT.Copy).then_inc(w_hi, 1)
            split_y(1)
            for i in range(tiles):
                act.wait_ge(var_done, i + 1)
                nc.scalar.activation(stat(i, 15, 16), stat(i, 14, 15), ACT.Sqrt).then_inc(root_done, 1)
                act.wait_ge(normed, i + 1)
                act.dma_start(out_rows(i), t_buf[i % 2]).then_inc(stored[i % 2], 16)
                if i + 2 < tiles:
                    split_y(i + 2)
            for s in range(2):
                act.wait_ge(stored[s], 16 * (tiles // 2))

        @block.vector
        def _(v):
            count = [0]

            def after(ins):
                count[0] += 1
                ins.then_inc(dve, 1)
                v.wait_ge(dve, count[0])

            def split_y(i):
                v.wait_ge(y_hi, i + 1)
                nc.vector.tensor_tensor(m.w_lo[:, i % 2, :, :], m.w_raw[:, i % 2, :, :], f(m.w_hi[:, i % 2, :, :]),
                                        ALU.subtract).then_inc(y_ready, 1)

            split_y(0)
            for k in range(KT):
                v.wait_ge(w_hi, k + 1)
                nc.vector.tensor_tensor(m.h_lo[:, k, 0:D], stage[k % 2], f(m.h_hi[:, k, 0:D]), ALU.subtract)\
                    .then_inc(w_ready, 1)
            v.wait_ge(rows_in, 16 * (3 + conds))
            for cnd in range(conds):
                nc.vector.scalar_tensor_tensor(gain[cnd], gain[cnd], 1.0, b_row, ALU.add, ALU.add).then_inc(gains, 1)
            split_y(1)
            v.wait_ge(gains, conds)
            for i in range(tiles):
                t, x = t_buf[i % 2], x_buf[i % 2]
                b = 2 * (i % 3)
                v.wait_ge(mm_done, i + 1)
                if i >= 2:
                    v.wait_ge(stored[i % 2], 16 * (i // 2))
                nc.vector.tensor_tensor(t, m.banks(b, 0, D), gain[i // LAT_TILES], ALU.mult).then_inc(psum_free, 1)
                v.wait_ge(psum_free, i + 1)
                v.wait_ge(x_loaded[i % 2], 16 * (i // 2 + 1))
                nc.vector.scalar_tensor_tensor(t, x, ALPHA, t, ALU.mult, ALU.add).then_inc(x_free, 1)
                v.wait_ge(x_free, i + 1)
                nc.vector.bn_stats(stat(i, 0, 6), t[:, 0:512])
                after(nc.vector.bn_stats(stat(i, 6, 12), t[:, 512:D]))
                after(nc.vector.bn_aggr(stat(i, 12, 14), stat(i, 0, 12)))
                nc.vector.tensor_scalar(stat(i, 14, 15), stat(i, 13, 14), EPS, None, ALU.add).then_inc(var_done, 1)
                v.wait_ge(root_done, i + 1)
                after(nc.vector.reciprocal(stat(i, 16, 17), stat(i, 15, 16)))
                after(nc.vector.tensor_scalar(t, t, stat(i, 12, 13), stat(i, 16, 17), ALU.subtract, ALU.mult))
                after(nc.vector.tensor_tensor(t, t, g_row, ALU.mult))
                nc.vector.tensor_tensor(t, t, beta_row, ALU.add).then_inc(normed, 1)
                if i + 2 < tiles:
                    split_y(i + 2)

        @block.tensor
        def _(pe):
            for i in range(tiles):
                pe.wait_ge(y_ready, i + 1)
                if i >= 3:
                    pe.wait_ge(psum_free, i - 2)
                for k in range(KT):
                    if i == 0:
                        pe.wait_ge(w_ready, k + 1)
                    for n, (yt, wt) in enumerate(((m.w_hi, m.h_hi), (m.w_hi, m.h_lo), (m.w_lo, m.h_hi))):
                        for half in range(2):
                            mm = nc.tensor.matmul(m.bank(2 * (i % 3) + half), yt[:, i % 2, k, :],
                                                  wt[:, k, half * 512:half * 512 + 512],
                                                  start=(k == 0 and n == 0), stop=(k == KT - 1 and n == 2))
                mm.then_inc(mm_done, 1)


def backbone(nc, x, ctx, cond, w_mod, b_cols, b_gate, w_in, w_out, ln_g, ln_b, rpb, lam, sub_g, ident, rope, masks, out):
    scratch = lambda n, s: nc.dram_tensor(n, s, F32, kind="Internal").ap()
    x1 = scratch("x1", (TOK, D))
    gate_rows = scratch("gate_rows", (DEPTH, 2, D))
    toeplitz = scratch("toeplitz", (HEADS, GRID_W, RPB_H, GRID_W))
    y_t = [scratch(f"y_t{l}", (D, TOK)) for l in range(DEPTH)]
    rows0 = lambda t: x[t * P:(t + 1) * P, :] if t < LAT_TILES else ctx[(t - LAT_TILES) * P:(t - LAT_TILES + 1) * P, :]
    rows1 = lambda t: x1[t * P:(t + 1) * P, :]
    with ExitStack() as stack:
        m = Memory(nc, stack)
        modulation(nc, m, stack, w_mod, cond, b_cols, lam, sub_g, ident, rpb, toeplitz, gate_rows)
        load_tokens(nc, m, stack, 0, rows0)
        neighbourhood(nc, m, stack, w_in, toeplitz, masks, y_t[0])
        project(nc, m, stack, 0, w_out, y_t[0], gate_rows, b_gate, ln_g, ln_b, rows0, rows1, TOK_TILES)
        load_tokens(nc, m, stack, 1, rows1)
        differential(nc, m, stack, w_in, rope, y_t[1])
        project(nc, m, stack, 1, w_out, y_t[1], gate_rows, b_gate, ln_g, ln_b, rows1,
                lambda t: out[t * P:(t + 1) * P, :], LAT_TILES)


def shape_constants():
    ident = np.eye(P, dtype=np.float32)
    n_freq = HD // 4
    inv = np.float32(10000.0) ** (-np.arange(n_freq, dtype=np.float32) / np.float32(n_freq))
    t = np.arange(SEQ)
    pos = np.stack([t // GRID_W, t % GRID_W]).astype(np.float32)
    dim = np.arange(P) % HD
    ang = pos[dim // 32] * inv[dim % 16].astype(np.float32)[:, None]
    sign = np.where(dim % 32 < 16, -1.0, 1.0).astype(np.float32)[:, None]
    rope = np.stack([np.cos(ang), np.sin(ang) * sign], axis=1).astype(np.float32)
    w = np.arange(P) % GRID_W
    start = np.clip(w - WIN_C // 2, 0, GRID_W - WIN_C)[:, None]
    j = np.arange(GRID_W)[None]
    cols = np.where((j >= start) & (j < start + WIN_C), 0.0, NEG).astype(np.float32)
    every = np.repeat(cols[:, None], SLOTS, axis=1)
    inner = np.repeat(cols[:, None], INNER, axis=1)
    inner[:GRID_W, INNER - 1] = NEG
    inner[GRID_W:, 0] = NEG
    masks = np.concatenate([every.reshape(P, -1), inner.reshape(P, -1)], axis=1)
    return ident, rope, np.ascontiguousarray(masks)


def kernel(x, c, ctx, c_ctx, w_mod, b_mod, w_in, w_out, ln_g, ln_b, na_rpb, diff_lambda, diff_subln_g):
    import concourse.bacc as bacc
    from concourse.bass_utils import run_bass_kernel_spmd

    a = np.ascontiguousarray
    ident, rope, masks = shape_constants()
    cond = a(np.stack([np.asarray(c)[0], np.asarray(c_ctx)]).reshape(2, KT, P).transpose(2, 0, 1))
    b_mod = np.asarray(b_mod)
    b_cols = a(b_mod[:, 0:2 * D].reshape(DEPTH, 2 * KT, P).transpose(2, 0, 1))
    arrays = {
        "x": a(np.asarray(x)[0]), "ctx": a(np.asarray(ctx)[0]), "cond": cond, "w_mod": a(w_mod), "b_cols": b_cols,
        "b_gate": a(b_mod[:, 2 * D:]), "w_in": a(w_in), "w_out": a(w_out), "ln_g": a(ln_g), "ln_b": a(ln_b),
        "rpb": a(np.pad(np.asarray(na_rpb)[0], ((0, 0), (0, 0), (PAD, PAD)))),
        "lam": a(np.asarray(diff_lambda)[0].reshape(-1)), "sub_g": a(np.asarray(diff_subln_g)[0].reshape(P, 1)),
        "ident": ident, "rope": rope, "masks": masks,
    }
    nc = bacc.Bacc("TRN2", target_bir_lowering=False, num_devices=1)
    args = [nc.dram_tensor("in_" + n, v.shape, mybir.dt.from_np(v.dtype), kind="ExternalInput").ap() for n, v in arrays.items()]
    out = nc.dram_tensor("out", (SEQ, D), F32, kind="ExternalOutput").ap()
    backbone(nc, *args, out)
    r = run_bass_kernel_spmd(nc, [{"in_" + n: v for n, v in arrays.items()}], core_ids=[0])
    return r.results[0]["out"].reshape(1, SEQ, D)
```

```python
import math
from contextlib import ExitStack

import concourse.bass as bass
import numpy as np
from concourse import mybir

P = 128
D = 1024
SEQ = 1024
CTX = 256
TOK = SEQ + CTX
KT = D // P
NCH = D // P
LAT_TILES, CTX_TILES = SEQ // P, CTX // P
TOK_TILES = LAT_TILES + CTX_TILES
DEPTH = 2
GRID_W = 64
ROWS = SEQ // GRID_W
WIN_R, WIN_C = 8, 16
HEADS = 16
HD = 64
PAD = 63 - (WIN_C - 1)
RPB_W = 2 * WIN_C - 1 + 2 * PAD
RPB_H = 2 * WIN_R - 1
SLOTS = RPB_H - 1
INNER = WIN_R + 1
EPS = 1e-5
ALPHA = (2.0 * DEPTH) ** 0.25
LAMBDA_INIT = 0.8 - 0.6 * math.exp(-0.3 * 1)
SCALE = HD ** -0.5
NEG = -1e30

F32 = mybir.dt.float32
F32R = mybir.dt.float32r
ALU = mybir.AluOpType
ACT = mybir.ActivationFunctionType
AX = mybir.AxisListType.X

GROUPS = [(0, 512), (512, 512), (1024, 256)]
BLOCKS = [2 * D, D, 0, 3 * D]
SWAP16 = [i ^ 16 for i in range(32)]


CREDIT = 1
AHEAD = 4


def f(ap):
    return ap.bitcast(F32)


class Memory:

    def __init__(self, nc, stack):
        def sb(name, shape, dt=F32):
            return stack.enter_context(nc.sbuf_tensor(name, shape, dt))

        self.h_hi = sb("h_hi", [P, KT, TOK], F32R)
        self.h_lo = sb("h_lo", [P, KT, TOK], F32R)
        self.w_raw = sb("w_raw", [P, 2, KT, P])
        self.w_hi = sb("w_hi", [P, 2, KT, P], F32R)
        self.w_lo = sb("w_lo", [P, 2, KT, P], F32R)
        self.q_stack = sb("q_stack", [P, 2, TOK], F32R)
        self.k_dup = sb("k_dup", [P, 2, 2, TOK], F32R)
        self.v = sb("v", [P, TOK_TILES, P])
        self.k_raw = sb("k_raw", [P, TOK])
        self.gate = sb("gate", [P, TOK])
        self.y = sb("y", [P, TOK])
        self.big = sb("big", [P, 5120])
        self.aux = sb("aux", [P, 4608])
        self.extra_prob = sb("extra_prob", [P, TOK])
        self.pt = sb("pt", [P, 4, 4 * P])
        self.ident = sb("ident", [P, P])
        self.mean_mat = sb("mean_mat", [P, P])
        self.mod_cols = sb("mod_cols", [P, DEPTH, 2, 2 * KT])
        self.b_cols = sb("b_cols", [P, DEPTH, 2 * KT])
        self.cond = sb("cond", [P, 2, KT])
        self.cond_act = sb("cond_act", [P, 2, KT])
        self.neg_lambda = sb("neg_lambda", [P, 1])
        self.sub_gain = sb("sub_gain", [P, 1])
        self.stats = sb("stats", [P, 96])
        self.psum = stack.enter_context(nc.psum_tensor("acc", [P, 8, 512], F32))

    def bank(self, b, width=512):
        return self.psum[:, b, 0:width]

    def banks(self, b, first, last):
        return self.psum[:, :, :].rearrange("p b n -> p (b n)")[:, b * 512 + first:b * 512 + last]


def rows_broadcast(ap_row, n):
    return bass.AP(ap_row.tensor, ap_row.offset, [[0, P], [1, n]])


def modulation(nc, m, stack, w_mod, cond_in, b_cols_in, lam_in, sub_in, ident_in, rpb, toeplitz, gate_rows):
    sem = lambda n: stack.enter_context(nc.semaphore("m_" + n))
    NS = 8
    PIECES = DEPTH * KT * 3
    small_in, lam_loaded, bands = sem("small_in"), sem("lam_loaded"), sem("bands")
    w_in = [sem(f"w_in{s}") for s in range(NS)]
    tanh_done, cond_ready, piece_used = sem("tanh"), sem("cond"), sem("used")
    row_ready, turned, cols_done = sem("row"), sem("turned"), sem("cols")
    gates_out, dve, lam_exp, mean_set = sem("gates_out"), sem("dve"), sem("lam_exp"), sem("mean_set")

    slots = [m.big[:, i * 1024:(i + 1) * 1024] for i in range(4)] + \
            [m.aux[:, i * 1024:(i + 1) * 1024] for i in range(4)]
    row_buf = [b[0:2, i * 512:(i + 1) * 512] for b in (m.k_raw, m.gate, m.y) for i in range(2)]
    lam = m.v[:, 0:2, :].rearrange("p a b -> p (a b)")
    lam_prod = m.v[:, 2, 0:HD]
    sums = m.stats[:, 0:4]

    with nc.Block() as block:
        @block.sync
        def _(sp):
            sp.dma_start(m.cond[:, :, :], cond_in).then_inc(small_in, 16)
            sp.dma_start(m.b_cols[:, :, :], b_cols_in).then_inc(small_in, 16)
            sp.dma_start(m.ident[:, :], ident_in).then_inc(small_in, 16)
            sp.dma_start(lam, rows_broadcast(lam_in, 4 * HD)).then_inc(lam_loaded, 16)
            sp.dma_start(m.sub_gain[:, :], sub_in).then_inc(lam_loaded, 16)
            for n in range(PIECES):
                l, k, j = n // (3 * KT), n // 3 % KT, n % 3
                if n >= NS:
                    sp.wait_ge(piece_used, n - NS + 1)
                sp.dma_start(slots[n % NS], w_mod[l, k * P:(k + 1) * P, j * 1024:(j + 1) * 1024])\
                    .then_inc(w_in[n % NS], 16)
            for l in range(DEPTH):
                sp.wait_ge(row_ready, 6 * (l + 1))
                for j in (4, 5):
                    sp.dma_start(gate_rows[l, :, (j - 4) * 512:(j - 3) * 512], row_buf[j])\
                        .then_inc(gates_out, 16)
            sp.wait_ge(gates_out, 64)

        @block.gpsimd
        def _(pool):
            for h in range(HEADS):
                src = rpb[h, :, 63:127]
                pool.dma_start(toeplitz[h].rearrange("w d j -> d w j"),
                               bass.AP(src.tensor, src.offset, [[RPB_W, RPB_H], [-1, GRID_W], [1, GRID_W]]))\
                    .then_inc(bands, 16)
            pool.wait_ge(bands, 16 * HEADS)

        @block.scalar
        def _(act):
            act.wait_ge(small_in, 48)
            nc.scalar.activation(m.cond_act[:, :, :], m.cond[:, :, :], ACT.Tanh, scale=0.5).then_inc(tanh_done, 1)
            act.wait_ge(dve, 2)
            nc.scalar.activation(sums[:, 2:4], sums[:, 0:2], ACT.Exp).then_inc(lam_exp, 1)

        @block.vector
        def _(v):
            v.wait_ge(tanh_done, 1)
            nc.vector.scalar_tensor_tensor(m.cond_act[:, :, :], m.cond_act[:, :, :], 1.0, m.cond[:, :, :],
                                           ALU.add, ALU.mult).then_inc(cond_ready, 1)
            nc.vector.memset(m.mean_mat[:, :], 1.0 / P).then_inc(mean_set, 1)
            v.wait_ge(lam_loaded, 32)
            for i in range(2):
                if i:
                    v.wait_ge(dve, 1)
                nc.vector.tensor_tensor_reduce(out=lam_prod, in0=lam[:, 2 * i * HD:(2 * i + 1) * HD],
                                               in1=lam[:, (2 * i + 1) * HD:(2 * i + 2) * HD], scale=1.0, scalar=0.0,
                                               op0=ALU.mult, op1=ALU.add, accum_out=sums[:, i:i + 1]).then_inc(dve, 1)
            v.wait_ge(lam_exp, 1)
            nc.vector.tensor_tensor(sums[:, 0:1], sums[:, 3:4], sums[:, 2:3], ALU.subtract).then_inc(dve, 1)
            v.wait_ge(dve, 3)
            nc.vector.tensor_scalar(m.neg_lambda[:, :], sums[:, 0:1], -LAMBDA_INIT, None, ALU.add).then_inc(dve, 1)
            nc.vector.tensor_scalar(m.sub_gain[:, :], m.sub_gain[:, :], 0.5 * (1.0 - LAMBDA_INIT), None, ALU.mult)\
                .then_inc(dve, 1)
            for l in range(DEPTH):
                v.wait_ge(piece_used, 3 * KT * (l + 1))
                if l:
                    v.wait_ge(turned, l)
                    v.wait_ge(gates_out, 32 * l)
                for j in range(6):
                    nc.vector.tensor_scalar(row_buf[j], m.psum[0:2, j, :], 0.5, None, ALU.mult).then_inc(row_ready, 1)
                v.wait_ge(turned, l + 1)
                cols = m.bank(6, 64).rearrange("p (k c) -> p c k", c=2)
                for cnd in range(2):
                    nc.vector.tensor_tensor(m.mod_cols[:, l, cnd, :], cols[:, cnd, 0:2 * KT], m.b_cols[:, l, :], ALU.add)\
                        .then_inc(cols_done, 1)
                    v.wait_ge(cols_done, 4 * l + 2 * cnd + 1)
                    nc.vector.tensor_scalar(m.mod_cols[:, l, cnd, KT:2 * KT], m.mod_cols[:, l, cnd, KT:2 * KT], 1.0,
                                            None, ALU.add).then_inc(cols_done, 1)

        @block.tensor
        def _(pe):
            pe.wait_ge(cond_ready, 1)
            for l in range(DEPTH):
                if l:
                    pe.wait_ge(row_ready, 6 * l)
                for k in range(KT):
                    for j in range(3):
                        n = (l * KT + k) * 3 + j
                        pe.wait_ge(w_in[n % NS], 16 * (n // NS + 1))
                        for half in range(2):
                            mm = nc.tensor.matmul(m.psum[0:2, 2 * j + half, :], m.cond_act[:, :, k],
                                                  slots[n % NS][:, half * 512:(half + 1) * 512],
                                                  start=(k == 0), stop=(k == KT - 1))
                        mm.then_inc(piece_used, 1)
                pe.wait_ge(row_ready, 6 * (l + 1))
                if l:
                    pe.wait_ge(cols_done, 4 * l)
                for k in range(2 * KT):
                    src = row_buf[k // 4][:, (k % 4) * P:(k % 4 + 1) * P]
                    mm = nc.tensor.transpose(m.psum[:, 6, 2 * k:2 * k + 2], src, m.ident[0:2, 0:2])
                mm.then_inc(turned, 1)


def load_tokens(nc, m, stack, l, rows):
    sem = lambda n: stack.enter_context(nc.semaphore(f"t{l}_" + n))
    loaded = [sem(f"loaded{g}") for g in range(3)]
    turned, modulated, hi_done, lo_done = sem("turned"), sem("modulated"), sem("hi"), sem("lo")
    TILES = [range(0, 4), range(4, 8), range(8, 10)]
    buf = [(m.big, m.aux, m.big)[g][:, 0:4096].rearrange("p (t n) -> p t n", t=4) for g in range(3)]
    tmp = [m.k_raw[:, 0:512], m.y[:, 0:512]]
    steps = [(g, k) for g in range(3) for k in range(KT)]

    with nc.Block() as block:
        @block.sync
        def _(sp):
            for g in range(3):
                if g == 2:
                    sp.wait_ge(turned, KT)
                for i, t in enumerate(TILES[g]):
                    sp.dma_start(buf[g][:, i, :], rows(t)).then_inc(loaded[g], 16)

        @block.tensor
        def _(pe):
            for n, (g, k) in enumerate(steps):
                if k == 0:
                    pe.wait_ge(loaded[g], 16 * len(TILES[g]))
                if n >= 4:
                    pe.wait_ge(modulated, n - 3)
                for i in range(len(TILES[g])):
                    mm = nc.tensor.transpose(m.psum[:, n % 4, i * P:(i + 1) * P], buf[g][:, i, k * P:(k + 1) * P],
                                             m.ident[:, :])
                mm.then_inc(turned, 1)

        @block.scalar
        def _(act):
            for n, (g, k) in enumerate(steps):
                w = GROUPS[g][1]
                cnd = g // 2
                act.wait_ge(turned, n + 1)
                if n >= 2:
                    act.wait_ge(lo_done, n - 1)
                nc.scalar.activation(tmp[n % 2][:, 0:w], m.bank(n % 4, w), ACT.Identity,
                                     scale=m.mod_cols[:, l, cnd, KT + k:KT + k + 1],
                                     bias=m.mod_cols[:, l, cnd, k:k + 1]).then_inc(modulated, 1)

        @block.vector
        def _(v):
            for n, (g, k) in enumerate(steps):
                t0, w = GROUPS[g]
                v.wait_ge(modulated, n + 1)
                nc.vector.tensor_copy(m.h_hi[:, k, t0:t0 + w], tmp[n % 2][:, 0:w]).then_inc(hi_done, 1)
                v.wait_ge(hi_done, n + 1)
                nc.vector.tensor_tensor(m.h_lo[:, k, t0:t0 + w], tmp[n % 2][:, 0:w], f(m.h_hi[:, k, t0:t0 + w]),
                                        ALU.subtract).then_inc(lo_done, 1)


class Projection:

    def __init__(self, nc, m, stack, l, w_in, rotary):
        self.counters = []

        def sem(n):
            self.counters.append(stack.enter_context(nc.semaphore(f"p{l}_" + n)))
            return self.counters[-1]

        self.nc, self.m, self.w_in, self.l, self.rotary = nc, m, w_in, l, rotary
        self.w_loaded = [sem("w_loaded0"), sem("w_loaded1")]
        self.w_hi, self.w_split, self.proj = sem("w_hi"), sem("w_split"), sem("proj")
        self.evac, self.gate_done = sem("evac"), sem("gate_done")
        self.tanh_done = sem("tanh")
        self.v_turned, self.v_ready = sem("v_turned"), sem("v_ready")
        self.k_own, self.k_ready, self.q_ready = sem("k_own"), sem("k_ready"), sem("q_ready")
        self.rot_shuffled, self.rot_scaled, self.dve = sem("rot_shuffled"), sem("rot_scaled"), sem("rot_dve")
        self.k_hi, self.q_hi = sem("k_hi"), sem("q_hi")
        lat_only = l == DEPTH - 1
        self.q_groups = 2 if lat_only else 3
        self.q_cols = SEQ if lat_only else TOK
        sizes = [3, 3, self.q_groups, self.q_groups]
        self.cum = [sum(sizes[:b + 1]) for b in range(4)]
        self.G = self.cum[-1]
        self.groups = [(b, g) for b in range(4) for g in range(sizes[b])]
        self.gate_groups = list(range(self.cum[2], self.G))
        self.early_gate = self.gate_groups[:-1]

    def give_credit(self, sp, counters):
        for s in self.counters + counters:
            sp.sem_inc(s, CREDIT)

    def load(self, sp, c, b):
        col = c * P + (BLOCKS[b % 4] + b // 4 * P)
        src = self.w_in[self.l].rearrange("(k p) n -> p k n", p=P)[:, :, bass.ds(col, P)]
        sp.dma_start(self.m.w_raw[:, b % 2, :, :], src).then_inc(self.w_loaded[b % 2], 16)

    def load_first(self, sp):
        self.load(sp, 0, 0)
        self.load(sp, 0, 1)
        for b in (2, 3):
            sp.wait_ge(self.w_split, CREDIT + (b - 1))
            self.load(sp, 0, b)

    def load_next(self, sp, c):
        for b in (4, 5, 6, 7):
            sp.wait_ge(self.w_split, CREDIT + c * 4 + (b - 1))
            self.load(sp, c, b)

    def split_hi_part(self, act, c, b):
        act.wait_ge(self.w_loaded[b % 2], CREDIT + c * 32 + 16 * (b // 2 + 1))
        if b >= 1:
            act.wait_ge(self.proj, CREDIT + c * self.G + ([0] + self.cum)[b - 1])
        self.nc.scalar.activation(self.m.w_hi[:, b % 2, :, :], self.m.w_raw[:, b % 2, :, :], ACT.Copy)\
            .then_inc(self.w_hi, 1)

    def split_lo_part(self, v, c, b):
        v.wait_ge(self.w_hi, CREDIT + c * 4 + (b + 1))
        self.nc.vector.tensor_tensor(self.m.w_lo[:, b % 2, :, :], self.m.w_raw[:, b % 2, :, :],
                                     f(self.m.w_hi[:, b % 2, :, :]), ALU.subtract).then_inc(self.w_split, 1)

    def bank_of(self, j):
        return j % 4 if j < self.cum[2] else 8 - self.G + j

    def product(self, pe, c, j):
        nc, m = self.nc, self.m
        b, g = self.groups[j]
        t0, w = GROUPS[g]
        if g == 0:
            pe.wait_ge(self.w_split, CREDIT + c * 4 + (b + 1))
        if AHEAD <= j < self.cum[2]:
            pe.wait_ge(self.evac, CREDIT + c * self.cum[2] + (j - 3))
        for k in range(KT):
            for i, (wt, ht) in enumerate(((m.w_hi, m.h_hi), (m.w_hi, m.h_lo), (m.w_lo, m.h_hi))):
                mm = nc.tensor.matmul(m.bank(self.bank_of(j), w), wt[:, b % 2, k, :], ht[:, k, t0:t0 + w],
                                      start=(k == 0 and i == 0), stop=(k == KT - 1 and i == 2))
        mm.then_inc(self.proj, 1)

    def turn_v(self, pe, c, g):
        t0, w = GROUPS[g]
        pe.wait_ge(self.evac, CREDIT + c * self.cum[2] + (g + 1))
        if g == 2:
            pe.wait_ge(self.v_ready, CREDIT + c * 3 + 1)
        for i in range(w // P):
            mm = self.nc.tensor.transpose(self.m.psum[:, 4 + g % 2, i * P:(i + 1) * P],
                                          self.m.k_raw[:, t0 + i * P:t0 + (i + 1) * P], self.m.ident[:, :])
        mm.then_inc(self.v_turned, 1)

    def pe_part(self, pe, c, gate_banks_free):
        self.turn_v(pe, c, 0)
        self.turn_v(pe, c, 1)
        self.product(pe, c, AHEAD)
        self.turn_v(pe, c, 2)
        for j in range(AHEAD + 1, self.cum[2]):
            self.product(pe, c, j)
        gate_banks_free(pe)
        for j in self.early_gate:
            self.product(pe, c, j)
        pe.wait_ge(self.q_ready, CREDIT + (c + 1) * 2 * self.q_groups)
        pe.wait_ge(self.k_ready, CREDIT + c * 2 + 2)

    def late_product(self, pe, c):
        self.product(pe, c, self.G - 1)

    def before_turns(self, pe, c):
        pe.wait_ge(self.gate_done, CREDIT + c * self.q_groups + len(self.early_gate))

    def before_values(self, pe, c):
        pe.wait_ge(self.gate_done, CREDIT + c * self.q_groups + self.q_groups)
        pe.wait_ge(self.v_ready, CREDIT + c * 3 + 3)

    def evacuate(self, act, c, j):
        b, g = self.groups[j]
        t0, w = GROUPS[g]
        dst = (self.m.k_raw, self.m.k_raw, self.m.y)[b]
        act.wait_ge(self.proj, CREDIT + c * self.G + (j + 1))
        if b == 1:
            act.wait_ge(self.v_turned, CREDIT + c * 3 + (g + 1))
        self.nc.scalar.activation(dst[:, t0:t0 + w], self.m.bank(self.bank_of(j), w), ACT.Copy,
                                  scale=SCALE if b == 2 else 1.0).then_inc(self.evac, 1)

    def evacuate_v(self, act, c, g):
        t0, w = GROUPS[g]
        act.wait_ge(self.v_turned, CREDIT + c * 3 + (g + 1))
        self.nc.scalar.activation(self.m.v[:, t0 // P:(t0 + w) // P, :],
                                  self.m.bank(4 + g % 2, w).rearrange("p (t n) -> p t n", n=P), ACT.Copy)\
            .then_inc(self.v_ready, 1)

    def duplicate_k(self, act, c):
        act.wait_ge(self.k_own, CREDIT + c * 2 + 2)
        for h in range(2):
            own, other = slice(64 * h, 64 * h + 64), slice(64 - 64 * h, 128 - 64 * h)
            self.nc.scalar.activation(self.m.k_dup[other, h, :, :], f(self.m.k_dup[own, h, :, :]), ACT.Copy)\
                .then_inc(self.k_ready, 1)

    def gate_tanh(self, act, c, j):
        t0, w = GROUPS[self.groups[j][1]]
        act.wait_ge(self.proj, CREDIT + c * self.G + (j + 1))
        self.nc.scalar.activation(self.m.gate[:, t0:t0 + w], self.m.bank(self.bank_of(j), w), ACT.Tanh, scale=0.5)\
            .then_inc(self.tanh_done, 1)

    def act_part(self, act, c, gate_free, y_free, last):
        self.split_hi_part(act, c, 2)
        self.evacuate_v(act, c, 0)
        self.evacuate(act, c, 3)
        self.evacuate_v(act, c, 1)
        self.evacuate_v(act, c, 2)
        self.evacuate(act, c, 4)
        self.evacuate(act, c, 5)
        self.split_hi_part(act, c, 3)
        y_free(act)
        for j in range(6, self.cum[2]):
            self.evacuate(act, c, j)
        self.duplicate_k(act, c)
        if not last:
            self.split_hi_part(act, c, 4)
        gate_free(act)
        for j in self.early_gate:
            self.gate_tanh(act, c, j)

    def late_tanh(self, act, c):
        self.gate_tanh(act, c, self.G - 1)

    def gate_silu(self, v, c, j):
        g = self.groups[j][1]
        t0, w = GROUPS[g]
        v.wait_ge(self.tanh_done, CREDIT + c * self.q_groups + (g + 1))
        self.nc.vector.scalar_tensor_tensor(self.m.gate[:, t0:t0 + w], self.m.gate[:, t0:t0 + w], 1.0,
                                            self.m.bank(self.bank_of(j), w), ALU.add, ALU.mult)\
            .then_inc(self.gate_done, 1)

    def rotate(self, v, c, x, block, g):
        a, n = GROUPS[g]
        turn = 2 * block + g
        cols = slice(a, a + n)
        rot, scaled = self.m.big[:, cols], self.m.big[:, SEQ + a:SEQ + a + n]
        self.nc.vector.tensor_tensor(scaled, x[:, cols], self.m.aux[:, cols], ALU.mult).then_inc(self.dve, 1)
        self.nc.vector.stream_shuffle(rot, x[:, cols], SWAP16).then_inc(self.rot_shuffled, 1)
        v.wait_ge(self.dve, CREDIT + c * 8 + (2 * turn + 1))
        v.wait_ge(self.rot_scaled, CREDIT + c * 4 + (turn + 1))
        self.nc.vector.tensor_tensor(x[:, cols], scaled, rot, ALU.add).then_inc(self.dve, 1)
        v.wait_ge(self.dve, CREDIT + c * 8 + (2 * turn + 2))

    def scale_partner(self, pool, c):
        for turn in range(4):
            a, n = GROUPS[turn % 2]
            rot, sin = self.m.big[:, a:a + n], self.m.aux[:, SEQ + a:SEQ + a + n]
            pool.wait_ge(self.rot_shuffled, CREDIT + c * 4 + (turn + 1))
            self.nc.gpsimd.tensor_tensor(rot, rot, sin, ALU.mult).then_inc(self.rot_scaled, 1)

    def split_k(self, v, c):
        m = self.m
        for g in range(3):
            if self.rotary and g < 2:
                v.wait_ge(self.evac, CREDIT + c * self.cum[2] + (self.cum[0] + g + 1))
                self.rotate(v, c, m.k_raw, 0, g)
        v.wait_ge(self.evac, CREDIT + c * self.cum[2] + self.cum[1])
        for h in range(2):
            own = slice(64 * h, 64 * h + 64)
            self.nc.vector.tensor_copy(m.k_dup[own, h, 0, :], m.k_raw[own, :]).then_inc(self.k_hi, 1)
        for h in range(2):
            own = slice(64 * h, 64 * h + 64)
            v.wait_ge(self.k_hi, CREDIT + c * 2 + (h + 1))
            self.nc.vector.tensor_tensor(m.k_dup[own, h, 1, :], m.k_raw[own, :], f(m.k_dup[own, h, 0, :]),
                                         ALU.subtract).then_inc(self.k_own, 1)

    def split_q(self, v, c):
        m, n = self.m, self.q_groups
        for g in range(n):
            t0, w = GROUPS[g]
            v.wait_ge(self.evac, CREDIT + c * self.cum[2] + (self.cum[1] + g + 1))
            if self.rotary:
                self.rotate(v, c, m.y, 1, g)
            for h in range(2):
                own = slice(64 * h, 64 * h + 64)
                self.nc.vector.tensor_copy(m.q_stack[own, h, t0:t0 + w], m.y[own, t0:t0 + w]).then_inc(self.q_hi, 1)
            for h in range(2):
                own, other = slice(64 * h, 64 * h + 64), slice(64 - 64 * h, 128 - 64 * h)
                v.wait_ge(self.q_hi, CREDIT + c * 2 * n + (2 * g + h + 1))
                self.nc.vector.tensor_tensor(m.q_stack[other, h, t0:t0 + w], m.y[own, t0:t0 + w],
                                             f(m.q_stack[own, h, t0:t0 + w]), ALU.subtract).then_inc(self.q_ready, 1)

    def dve_part(self, v, c, last):
        self.split_lo_part(v, c, 2)
        self.split_k(v, c)
        self.split_lo_part(v, c, 3)
        self.split_q(v, c)
        if not last:
            self.split_lo_part(v, c, 4)
        for j in self.early_gate:
            self.gate_silu(v, c, j)

    def late_silu(self, v, c):
        self.gate_silu(v, c, self.G - 1)


def each_chunk(engine, chunk):
    with engine.Fori(0, NCH - 1) as c:
        chunk(c, False)
    chunk(NCH - 1, True)


class Item:

    def __init__(self, head, qt):
        self.head, self.qt = head, qt
        self.local = qt < LAT_TILES
        self.rows = 0
        if self.local:
            r = 2 * qt
            start = [min(max(x - WIN_R // 2, 0), ROWS - WIN_R) for x in (r, r + 1)]
            self.k0 = start[0]
            self.rows = start[1] + WIN_R - start[0]
            self.slot = self.k0 - r + WIN_R - 2
        self.width = CTX + self.rows * GRID_W
        tiles = [LAT_TILES + i for i in range(CTX_TILES)]
        if self.local:
            tiles += [self.k0 // 2 + i for i in range((self.rows + 1) // 2)]
        self.key_tiles = tiles
        self.y_group = head * 3 + qt // 4


def neighbourhood(nc, m, stack, w_in, toeplitz, masks_in, y_out):
    l = 0
    p = Projection(nc, m, stack, l, w_in, rotary=False)
    counters = []

    def sem(n):
        counters.append(stack.enter_context(nc.semaphore("n_" + n)))
        return counters[-1]

    masks_loaded = stack.enter_context(nc.semaphore("n_masks"))
    bias_loaded, bias_ready, bias_tmp = sem("bias_loaded"), sem("bias_ready"), sem("bias_tmp")
    s_done, raw_max, max_done = sem("s_done"), sem("raw_max"), sem("max_done")
    exp_done, recip_done, p_ready = sem("exp_done"), sem("recip"), sem("p_ready")
    turned, pt_ready, av_done, y_ready, y_stored = sem("turned"), sem("pt_ready"), sem("av_done"), sem("y_ready"), sem("y_stored")
    pad_set = stack.enter_context(nc.semaphore("n_pad"))

    items = [Item(h, qt) for h in range(2) for qt in range(TOK_TILES)]
    NI = len(items)
    NL = sum(it.local for it in items)
    WMAX = CTX + (INNER + 1) * GRID_W
    PB = 4
    prob = m.big[:, 0:PB * WMAX].rearrange("p (b n) -> p b n", b=PB)
    mask_w = SLOTS * GRID_W
    inner_w = INNER * GRID_W
    mask = m.aux[:, 0:mask_w + inner_w]
    mask_all, mask_inner = mask[:, 0:mask_w], mask[:, mask_w:]
    bias = m.aux[:, 1536:1536 + 2 * mask_w].rearrange("p (h n) -> p h n", h=2)
    bias_inner = m.aux[:, 1536 + 2 * mask_w:1536 + 2 * (mask_w + inner_w)].rearrange("p (h n) -> p h n", h=2)
    turns = [(i, a, min(4, len(it.key_tiles) - a)) for i, it in enumerate(items) for a in range(0, len(it.key_tiles), 4)]
    of_item = [[n for n, t in enumerate(turns) if t[0] == i] for i in range(NI)]
    NT = len(turns)
    YG = 6
    last_item = [max(i for i, it in enumerate(items) if it.y_group == g) for g in range(YG)]
    local_before = [sum(x.local for x in items[:i]) for i in range(NI + 1)]
    assert NI % 2 == 0 and NT % 6 == 0 and NI % PB == 0

    def stat(i, col):
        return m.stats[:, (i % 4) * 8 + col:(i % 4) * 8 + col + 1]

    with nc.Block() as block:
        @block.sync
        def _(sp):
            p.give_credit(sp, counters)
            sp.dma_start(mask, masks_in).then_inc(masks_loaded, 16)
            p.load_first(sp)

            def chunk(c, last):
                sp.wait_ge(max_done, CREDIT + c * NI)
                for half in range(2):
                    src = toeplitz[bass.ds(c * 2, 2), :, 1 - half:1 - half + SLOTS, :].rearrange("h w d j -> w h (d j)")
                    sp.dma_start(bias[64 * half:64 * half + 64, :, :], src).then_inc(bias_loaded, 16)
                if not last:
                    p.load_next(sp, c)
                sp.wait_ge(y_ready, CREDIT + c * YG + YG)
                sp.dma_start(y_out[bass.ds(c * P, P), :], m.y[:, :]).then_inc(y_stored, 16)

            each_chunk(sp, chunk)
            sp.wait_ge(y_stored, CREDIT + 16 * NCH)

        @block.gpsimd
        def _(pool):
            nc.gpsimd.memset(prob[:, :, WMAX - GRID_W:WMAX], 0.0).then_inc(pad_set, 1)
            pool.wait_ge(masks_loaded, 16)
            with pool.Fori(0, NCH) as c:
                pool.wait_ge(bias_loaded, CREDIT + c * 32 + 32)
                for h in range(2):
                    nc.gpsimd.tensor_tensor(bias_inner[:, h, :], bias[:, h, 2 * GRID_W:2 * GRID_W + inner_w], mask_inner,
                                            ALU.add).then_inc(bias_tmp, 1)
                for h in range(2):
                    pool.wait_ge(bias_tmp, CREDIT + c * 2 + (h + 1))
                    nc.gpsimd.tensor_tensor(bias[:, h, :], bias[:, h, :], mask_all, ALU.add).then_inc(bias_ready, 1)

        @block.scalar
        def _(act):
            p.split_hi_part(act, 0, 0)
            p.split_hi_part(act, 0, 1)
            for j in range(3):
                p.evacuate(act, 0, j)
            act.wait_ge(pad_set, 1)

            def chunk(c, last):
                def exp(i):
                    it = items[i]
                    act.wait_ge(max_done, CREDIT + c * NI + (i + 1))
                    nc.scalar.activation(prob[:, i % PB, 0:it.width], m.banks(2 * (i % 2), 0, it.width), ACT.Exp,
                                         bias=stat(i, 2), accum_out=stat(i, 3)).then_inc(exp_done, 1)

                def evac(n):
                    w = turns[n][2] * P
                    act.wait_ge(turned, CREDIT + c * NT + (n + 1))
                    act.wait_ge(av_done, CREDIT + c * NT + max(n - 2, 0))
                    nc.scalar.activation(m.pt[:, n % 3, 0:w], m.bank(4 + n % 2, w), ACT.Copy).then_inc(pt_ready, 1)

                p.act_part(act, c, lambda e: e.wait_ge(y_ready, CREDIT + c * YG), lambda e: e.wait_ge(y_stored, CREDIT + c * 16),
                           last)
                exp(0)
                p.late_tanh(act, c)
                for i in range(NI):
                    if i + 1 < NI:
                        exp(i + 1)
                    for n in of_item[i]:
                        evac(n)
                    if i == NI // 2 and not last:
                        p.split_hi_part(act, c, 5)
                if not last:
                    for j in range(3):
                        p.evacuate(act, c + 1, j)

            each_chunk(act, chunk)

        @block.vector
        def _(v):
            p.split_lo_part(v, 0, 0)
            p.split_lo_part(v, 0, 1)

            def chunk(c, last):
                def row_max(i):
                    it = items[i]
                    s = 2 * (i % 2)
                    v.wait_ge(s_done, CREDIT + c * NI + (i + 1))
                    if not it.local:
                        nc.vector.reduce_max(stat(i, 2), m.banks(s, 0, CTX), AX, negate=True).then_inc(max_done, 1)
                        return
                    nl = local_before[i]
                    nc.vector.reduce_max(stat(i, 0), m.banks(s, 0, CTX), AX)
                    if it.rows == INNER:
                        b = bias_inner[:, it.head, :]
                    else:
                        b = bias[:, it.head, it.slot * GRID_W:(it.slot + WIN_R) * GRID_W]
                    loc = m.banks(s, CTX, it.width)
                    nc.vector.tensor_tensor_reduce(out=loc, in0=loc, in1=b, scale=1.0, scalar=-3e38, op0=ALU.add,
                                                   op1=ALU.max, accum_out=stat(i, 1)).then_inc(raw_max, 1)
                    v.wait_ge(raw_max, CREDIT + c * NL + (nl + 1))
                    nc.vector.reduce_max(stat(i, 2), m.stats[:, (i % 4) * 8:(i % 4) * 8 + 2], AX, negate=True)\
                        .then_inc(max_done, 1)

                def normalise(i):
                    it = items[i]
                    v.wait_ge(exp_done, CREDIT + c * NI + (i + 1))
                    nc.vector.reciprocal(stat(i, 4), stat(i, 3)).then_inc(recip_done, 1)
                    v.wait_ge(recip_done, CREDIT + c * NI + (i + 1))
                    pr = prob[:, i % PB, 0:it.width]
                    nc.vector.tensor_scalar(pr, pr, stat(i, 4), None, ALU.mult).then_inc(p_ready, 1)

                def gate_y(g):
                    h, t0 = g // 3, (g % 3) * 512
                    w = min(512, TOK - t0)
                    own = slice(64 * h, 64 * h + 64)
                    v.wait_ge(av_done, CREDIT + c * NT + (of_item[last_item[g]][-1] + 1))
                    nc.vector.scalar_tensor_tensor(m.y[own, t0:t0 + w], m.psum[own, 6 + g % 2, 0:w], 0.5,
                                                   m.gate[own, t0:t0 + w], ALU.mult, ALU.mult).then_inc(y_ready, 1)

                p.dve_part(v, c, last)
                v.wait_ge(bias_ready, CREDIT + c * 2 + 2)
                row_max(0)
                row_max(1)
                p.late_silu(v, c)
                for i in range(NI):
                    normalise(i)
                    if i + 2 < NI:
                        row_max(i + 2)
                    if i - 2 in last_item:
                        gate_y(last_item.index(i - 2))
                    if i == NI // 2 and not last:
                        p.split_lo_part(v, c, 5)
                for g in range(YG):
                    if last_item[g] + 2 >= NI:
                        gate_y(g)

            each_chunk(v, chunk)

        @block.tensor
        def _(pe):
            for j in range(AHEAD):
                p.product(pe, 0, j)

            def chunk(c, last):
                def scores(i):
                    it = items[i]
                    s = 2 * (i % 2)
                    if i >= 2:
                        pe.wait_ge(exp_done, CREDIT + c * NI + (i - 1))
                    parts = [(s, 0, CTX, SEQ)]
                    if it.local:
                        k0 = it.k0 * GRID_W
                        parts += [(s, CTX, 256, k0), (s + 1, 0, (it.rows - 4) * GRID_W, k0 + 256)]
                    for b, col, w, key in parts:
                        for part in range(2):
                            mm = nc.tensor.matmul(m.psum[:, b, col:col + w], m.q_stack[:, it.head, it.qt * P:(it.qt + 1) * P],
                                                  m.k_dup[:, it.head, part, key:key + w], start=(part == 0), stop=(part == 1))
                    mm.then_inc(s_done, 1)

                def turn(n):
                    i, a, cnt = turns[n]
                    pe.wait_ge(p_ready, CREDIT + c * NI + (i + 1))
                    if n >= 2:
                        pe.wait_ge(pt_ready, CREDIT + c * NT + (n - 1))
                    for t in range(cnt):
                        mm = nc.tensor.transpose(m.psum[:, 4 + n % 2, t * P:(t + 1) * P],
                                                 prob[:, i % PB, (a + t) * P:(a + t + 1) * P], m.ident[:, :])
                    mm.then_inc(turned, 1)

                def values(n):
                    i, a, cnt = turns[n]
                    it = items[i]
                    if n == 0:
                        p.before_values(pe, c)
                    pe.wait_ge(pt_ready, CREDIT + c * NT + (n + 1))
                    if a == 0 and it.qt % 4 == 0:
                        pe.wait_ge(y_ready, CREDIT + c * YG + max(it.y_group - 1, 0))
                    for t in range(cnt):
                        mm = nc.tensor.matmul(m.psum[:, 6 + it.y_group % 2, (it.qt % 4) * P:(it.qt % 4 + 1) * P],
                                              m.v[:, it.key_tiles[a + t], :], m.pt[:, n % 3, t * P:(t + 1) * P],
                                              start=(a + t == 0), stop=(a + t == len(it.key_tiles) - 1))
                    mm.then_inc(av_done, 1)

                def ahead(j):
                    if not last:
                        pe.wait_ge(exp_done, CREDIT + c * NI + (NI - 1 if j < 2 else NI))
                        p.product(pe, c + 1, j)

                p.pe_part(pe, c, lambda e: e.wait_ge(y_ready, CREDIT + c * YG))
                scores(0)
                scores(1)
                p.late_product(pe, c)
                p.before_turns(pe, c)
                for i in range(NI + 1):
                    if i + 2 < NI:
                        scores(i + 2)
                    else:
                        ahead(i + 2 - NI)
                    new = of_item[i] if i < NI else []
                    old = of_item[i - 1] if i else []
                    for n in range(2):
                        if n < len(new):
                            turn(new[n])
                        if n < len(old):
                            values(old[n])
                ahead(3)

            each_chunk(pe, chunk)


def differential(nc, m, stack, w_in, rope_in, y_out):
    l = 1
    p = Projection(nc, m, stack, l, w_in, rotary=True)
    counters = []

    def sem(n):
        counters.append(stack.enter_context(nc.semaphore("d_" + n)))
        return counters[-1]

    rope_loaded = stack.enter_context(nc.semaphore("d_rope"))
    s_done, max_done, exp_done, coef, p_ready = sem("s_done"), sem("max_done"), sem("exp_done"), sem("coef"), sem("p_ready")
    turned, pt_ready, av_done = sem("turned"), sem("pt_ready"), sem("av_done")
    y_raw, sq_done, ms_done, var_done = sem("y_raw"), sem("sq_done"), sem("ms_done"), sem("var_done")
    root_done, inv_done, diag_ready, spread = sem("root_done"), sem("inv_done"), sem("diag_ready"), sem("spread")
    y_ready, y_stored, fin = sem("y_ready"), sem("y_stored"), sem("fin")

    NQ = LAT_TILES
    KEYS = TOK_TILES
    turns = [(t, a, min(4, KEYS - a)) for t in range(NQ) for a in range(0, KEYS, 4)]
    TPT = 3
    NT = len(turns)
    bufs = [m.big[:, i * TOK:(i + 1) * TOK] for i in range(4)] + [m.extra_prob[:, :]]
    prob = lambda mp, t: bufs[t % 3] if mp == 0 else bufs[3 + t % 2]
    y_sb, sq = m.aux[:, 2048:3072], m.aux[:, 3072:4096]
    stat = lambda t, col: m.stats[:, (t % 2) * 8 + col:(t % 2) * 8 + col + 1]
    eps_col = lambda t: m.stats[:, 32 + t:33 + t]
    variances, roots, inv_rms = (m.stats[:, 40 + i * NQ:40 + (i + 1) * NQ] for i in range(3))

    with nc.Block() as block:
        @block.sync
        def _(sp):
            p.give_credit(sp, counters)
            sp.dma_start(m.aux[:, 0:2 * SEQ].rearrange("p (a n) -> p a n", a=2), rope_in).then_inc(rope_loaded, 16)
            p.load_first(sp)

            def chunk(c, last):
                if not last:
                    p.load_next(sp, c)
                sp.wait_ge(y_ready, CREDIT + c * 2 + 2)
                sp.dma_start(y_out[bass.ds(c * P, P), 0:SEQ], m.y[:, 0:SEQ]).then_inc(y_stored, 16)

            each_chunk(sp, chunk)
            sp.wait_ge(y_stored, CREDIT + 16 * NCH)

        @block.gpsimd
        def _(pool):
            pool.wait_ge(rope_loaded, 16)
            with pool.Fori(0, NCH) as c:
                p.scale_partner(pool, c)

        @block.scalar
        def _(act):
            p.split_hi_part(act, 0, 0)
            p.split_hi_part(act, 0, 1)
            for j in range(3):
                p.evacuate(act, 0, j)

            def chunk(c, last):
                def exp(mp, t):
                    act.wait_ge(max_done, CREDIT + c * 2 * NQ + (2 * t + mp + 1))
                    nc.scalar.activation(prob(mp, t), m.banks(3 * mp, 0, TOK), ACT.Exp,
                                         bias=stat(t, mp), accum_out=stat(t, 2 + mp)).then_inc(exp_done, 1)

                def evac(n):
                    w = turns[n][2] * P
                    act.wait_ge(turned, CREDIT + c * NT + (n + 1))
                    act.wait_ge(av_done, CREDIT + c * NT + max(n - 3, 0))
                    nc.scalar.activation(m.pt[:, n % 4, 0:w], m.bank(6, w), ACT.Copy).then_inc(pt_ready, 1)

                def take_y(half):
                    cols = slice(half * 512, half * 512 + 512)
                    act.wait_ge(av_done, CREDIT + c * NT + 4 * TPT * (half + 1))
                    nc.scalar.activation(y_sb[:, cols], m.bank(7), ACT.Copy).then_inc(y_raw, 1)
                    act.wait_ge(y_raw, CREDIT + c * 2 + (half + 1))
                    nc.scalar.activation(sq[:, cols], y_sb[:, cols], ACT.Square).then_inc(sq_done, 1)

                p.act_part(act, c, lambda e: e.wait_ge(y_ready, CREDIT + c * 2), lambda e: e.wait_ge(y_stored, CREDIT + c * 16),
                           last)
                exp(0, 0)
                exp(1, 0)
                p.late_tanh(act, c)
                exp(0, 1)
                evac(0)
                exp(1, 1)
                for t in range(NQ):
                    if t == 4:
                        take_y(0)
                    evac(TPT * t + 1)
                    if t + 2 < NQ:
                        exp(0, t + 2)
                    evac(TPT * t + 2)
                    if t + 1 < NQ:
                        evac(TPT * t + 3)
                    if t + 2 < NQ:
                        exp(1, t + 2)
                    if t == 3 and not last:
                        p.split_hi_part(act, c, 5)
                take_y(1)
                if not last:
                    for j in range(3):
                        p.evacuate(act, c + 1, j)
                act.wait_ge(var_done, CREDIT + c * 1 + 1)
                nc.scalar.activation(roots, variances, ACT.Sqrt).then_inc(root_done, 1)

            each_chunk(act, chunk)

        @block.vector
        def _(v):
            p.split_lo_part(v, 0, 0)
            p.split_lo_part(v, 0, 1)
            v.wait_ge(rope_loaded, 16)

            def chunk(c, last):
                def row_max(mp, t):
                    v.wait_ge(s_done, CREDIT + c * 2 * NQ + (2 * t + mp + 1))
                    nc.vector.reduce_max(stat(t, mp), m.banks(3 * mp, 0, TOK), AX, negate=True).then_inc(max_done, 1)

                def combine(t):
                    v.wait_ge(exp_done, CREDIT + c * 2 * NQ + (2 * t + 2))
                    nc.vector.reciprocal(stat(t, 4), stat(t, 3)).then_inc(coef, 1)
                    nc.vector.tensor_scalar(eps_col(t), stat(t, 2), stat(t, 2), EPS, ALU.mult, ALU.mult).then_inc(coef, 1)
                    v.wait_ge(coef, CREDIT + c * 3 * NQ + (3 * t + 2))
                    nc.vector.tensor_scalar(stat(t, 5), stat(t, 2), stat(t, 4), m.neg_lambda[:, :], ALU.mult, ALU.mult)\
                        .then_inc(coef, 1)
                    v.wait_ge(coef, CREDIT + c * 3 * NQ + (3 * t + 3))
                    e0, e1 = prob(0, t), prob(1, t)
                    nc.vector.scalar_tensor_tensor(e0, e1, stat(t, 5), e0, ALU.mult, ALU.add).then_inc(p_ready, 1)

                def root_mean_square():
                    v.wait_ge(ms_done, CREDIT + c * NQ + NQ)
                    nc.vector.tensor_tensor(variances, m.bank(6, NQ), m.stats[:, 32:32 + NQ], ALU.add).then_inc(var_done, 1)
                    v.wait_ge(root_done, CREDIT + c * 1 + 1)
                    nc.vector.reciprocal(inv_rms, roots).then_inc(inv_done, 1)
                    v.wait_ge(inv_done, CREDIT + c * 1 + 1)
                    for t in range(NQ):
                        nc.vector.tensor_scalar(sq[:, t * P:(t + 1) * P], m.ident[:, :], inv_rms[:, t:t + 1], float(P),
                                                ALU.mult, ALU.mult).then_inc(diag_ready, 1)

                def finish(half):
                    cols = slice(half * 512, half * 512 + 512)
                    v.wait_ge(spread, CREDIT + c * 2 + (half + 1))
                    nc.vector.scalar_tensor_tensor(y_sb[:, cols], y_sb[:, cols], m.sub_gain[:, :], m.bank(6 + half),
                                                   ALU.mult, ALU.mult).then_inc(fin, 1)
                    v.wait_ge(fin, CREDIT + c * 2 + (half + 1))
                    nc.vector.tensor_tensor(m.y[:, cols], y_sb[:, cols], m.gate[:, cols], ALU.mult).then_inc(y_ready, 1)

                p.dve_part(v, c, last)
                row_max(0, 0)
                row_max(1, 0)
                combine(0)
                for t in range(NQ):
                    if t + 1 < NQ:
                        row_max(0, t + 1)
                    if t == 0:
                        p.late_silu(v, c)
                    if t:
                        combine(t)
                    if t + 1 < NQ:
                        row_max(1, t + 1)
                    if t == 4 and not last:
                        p.split_lo_part(v, c, 5)
                root_mean_square()
                finish(0)
                finish(1)

            each_chunk(v, chunk)

        @block.tensor
        def _(pe):
            for j in range(AHEAD):
                p.product(pe, 0, j)

            def chunk(c, last):
                def scores(mp, t):
                    if t:
                        pe.wait_ge(exp_done, CREDIT + c * 2 * NQ + (2 * (t - 1) + mp + 1))
                    for g, (k0, w) in enumerate(GROUPS):
                        for part in range(2):
                            mm = nc.tensor.matmul(m.bank(3 * mp + g, w), m.q_stack[:, mp, t * P:(t + 1) * P],
                                                  m.k_dup[:, mp, part, k0:k0 + w], start=(part == 0), stop=(part == 1))
                    mm.then_inc(s_done, 1)

                def turn(n):
                    t, a, cnt = turns[n]
                    pe.wait_ge(p_ready, CREDIT + c * NQ + (t + 1))
                    pe.wait_ge(pt_ready, CREDIT + c * NT + n)
                    for i in range(cnt):
                        mm = nc.tensor.transpose(m.psum[:, 6, i * P:(i + 1) * P],
                                                 prob(0, t)[:, (a + i) * P:(a + i + 1) * P], m.ident[:, :])
                    mm.then_inc(turned, 1)

                def values(n):
                    t, a, cnt = turns[n]
                    if n == 0:
                        p.before_values(pe, c)
                    pe.wait_ge(pt_ready, CREDIT + c * NT + (n + 1))
                    if a == 0 and t % 4 == 0:
                        pe.wait_ge(y_raw, CREDIT + c * 2 + t // 4)
                    for i in range(cnt):
                        mm = nc.tensor.matmul(m.psum[:, 7, (t % 4) * P:(t % 4 + 1) * P], m.v[:, a + i, :],
                                              m.pt[:, n % 4, i * P:(i + 1) * P], start=(a + i == 0), stop=(a + i == KEYS - 1))
                    mm.then_inc(av_done, 1)

                def ahead(j):
                    if not last:
                        pe.wait_ge(exp_done, CREDIT + c * 2 * NQ + (2 * NQ - 1 if j < 3 else 2 * NQ))
                        p.product(pe, c + 1, j)

                p.pe_part(pe, c, lambda e: e.wait_ge(y_ready, CREDIT + c * 2))
                scores(0, 0)
                scores(1, 0)
                p.late_product(pe, c)
                scores(0, 1)
                scores(1, 1)
                p.before_turns(pe, c)
                for t in range(NQ):
                    turn(TPT * t)
                    if t + 2 < NQ:
                        scores(0, t + 2)
                    else:
                        ahead(t + 2 - NQ)
                    if t:
                        values(TPT * t - 1)
                    turn(TPT * t + 1)
                    if t + 2 < NQ:
                        scores(1, t + 2)
                    values(TPT * t)
                    turn(TPT * t + 2)
                    values(TPT * t + 1)
                values(NT - 1)
                ahead(2)
                pe.wait_ge(sq_done, CREDIT + c * 2 + 2)
                for t in range(NQ):
                    nc.tensor.matmul(m.psum[:, 6, t:t + 1], sq[:, t * P:(t + 1) * P], m.mean_mat[:, 0:1],
                                     start=True, stop=True).then_inc(ms_done, 1)
                ahead(3)
                for half in range(2):
                    pe.wait_ge(diag_ready, CREDIT + c * NQ + 4 * (half + 1))
                    nc.tensor.matmul(m.bank(6 + half), m.mean_mat[:, :], sq[:, half * 512:half * 512 + 512],
                                     start=True, stop=True).then_inc(spread, 1)

            each_chunk(pe, chunk)


def project(nc, m, stack, l, w_out, y_in, gate_rows, b_gate, ln_g, ln_b, rows, out_rows, tiles):
    sem = lambda n: stack.enter_context(nc.semaphore(f"o{l}_" + n))
    w_loaded, y_loaded, x_loaded = ([sem(f"{n}{s}") for s in range(2)] for n in ("w", "y", "x"))
    stored = [sem(f"stored{s}") for s in range(2)]
    w_hi, w_ready, y_hi, y_ready, mm_done = sem("w_hi"), sem("w_ready"), sem("y_hi"), sem("y_ready"), sem("mm_done")
    rows_in, gains, dve, psum_free, x_free = sem("rows_in"), sem("gains"), sem("dve"), sem("psum_free"), sem("x_free")
    var_done, root_done, normed = sem("var"), sem("root"), sem("normed")

    stage = [m.k_raw[:, 0:D], m.gate[:, 0:D]]
    x_buf = [m.big[:, s * D:(s + 1) * D] for s in range(2)]
    t_buf = [m.big[:, (2 + s) * D:(3 + s) * D] for s in range(2)]
    b_row = m.big[:, 4 * D:5 * D]
    gain = [m.aux[:, s * D:(s + 1) * D] for s in range(2)]
    g_row, beta_row = m.aux[:, 2 * D:3 * D], m.aux[:, 3 * D:4 * D]
    conds = 2 if tiles > LAT_TILES else 1

    def stat(i, a, b):
        return m.stats[:, (i % 2) * 24 + a:(i % 2) * 24 + b]

    with nc.Block() as block:
        @block.sync
        def _(sp):
            for cnd in range(conds):
                sp.dma_start(gain[cnd], rows_broadcast(gate_rows[l, cnd, :], D)).then_inc(rows_in, 16)
            sp.dma_start(b_row, rows_broadcast(b_gate[l, :], D)).then_inc(rows_in, 16)
            sp.dma_start(g_row, rows_broadcast(ln_g[l, :], D)).then_inc(rows_in, 16)
            sp.dma_start(beta_row, rows_broadcast(ln_b[l, :], D)).then_inc(rows_in, 16)
            for k in range(KT):
                if k >= 2:
                    sp.wait_ge(w_ready, k - 1)
                sp.dma_start(stage[k % 2], w_out[l, k * P:(k + 1) * P, :]).then_inc(w_loaded[k % 2], 16)

        @block.gpsimd
        def _(pool):
            for i in range(tiles):
                if i >= 2:
                    pool.wait_ge(y_ready, i - 1)
                pool.dma_start(m.w_raw[:, i % 2, :, :],
                               y_in.rearrange("(k p) n -> p k n", p=P)[:, :, i * P:(i + 1) * P])\
                    .then_inc(y_loaded[i % 2], 16)
                if i >= 2:
                    pool.wait_ge(x_free, i - 1)
                pool.dma_start(x_buf[i % 2], rows(i)).then_inc(x_loaded[i % 2], 16)

        @block.scalar
        def _(act):
            def split_y(i):
                act.wait_ge(y_loaded[i % 2], 16 * (i // 2 + 1))
                if i >= 2:
                    act.wait_ge(mm_done, i - 1)
                nc.scalar.activation(m.w_hi[:, i % 2, :, :], m.w_raw[:, i % 2, :, :], ACT.Copy).then_inc(y_hi, 1)

            split_y(0)
            for k in range(KT):
                act.wait_ge(w_loaded[k % 2], 16 * (k // 2 + 1))
                nc.scalar.activation(m.h_hi[:, k, 0:D], stage[k % 2], ACT.Copy).then_inc(w_hi, 1)
            split_y(1)
            for i in range(tiles):
                act.wait_ge(var_done, i + 1)
                nc.scalar.activation(stat(i, 15, 16), stat(i, 14, 15), ACT.Sqrt).then_inc(root_done, 1)
                act.wait_ge(normed, i + 1)
                act.dma_start(out_rows(i), t_buf[i % 2]).then_inc(stored[i % 2], 16)
                if i + 2 < tiles:
                    split_y(i + 2)
            for s in range(2):
                act.wait_ge(stored[s], 16 * (tiles // 2))

        @block.vector
        def _(v):
            count = [0]

            def after(ins):
                count[0] += 1
                ins.then_inc(dve, 1)
                v.wait_ge(dve, count[0])

            def split_y(i):
                v.wait_ge(y_hi, i + 1)
                nc.vector.tensor_tensor(m.w_lo[:, i % 2, :, :], m.w_raw[:, i % 2, :, :], f(m.w_hi[:, i % 2, :, :]),
                                        ALU.subtract).then_inc(y_ready, 1)

            split_y(0)
            for k in range(KT):
                v.wait_ge(w_hi, k + 1)
                nc.vector.tensor_tensor(m.h_lo[:, k, 0:D], stage[k % 2], f(m.h_hi[:, k, 0:D]), ALU.subtract)\
                    .then_inc(w_ready, 1)
            v.wait_ge(rows_in, 16 * (3 + conds))
            for cnd in range(conds):
                nc.vector.scalar_tensor_tensor(gain[cnd], gain[cnd], 1.0, b_row, ALU.add, ALU.add).then_inc(gains, 1)
            split_y(1)
            v.wait_ge(gains, conds)
            for i in range(tiles):
                t, x = t_buf[i % 2], x_buf[i % 2]
                b = 2 * (i % 3)
                v.wait_ge(mm_done, i + 1)
                if i >= 2:
                    v.wait_ge(stored[i % 2], 16 * (i // 2))
                nc.vector.tensor_tensor(t, m.banks(b, 0, D), gain[i // LAT_TILES], ALU.mult).then_inc(psum_free, 1)
                v.wait_ge(psum_free, i + 1)
                v.wait_ge(x_loaded[i % 2], 16 * (i // 2 + 1))
                nc.vector.scalar_tensor_tensor(t, x, ALPHA, t, ALU.mult, ALU.add).then_inc(x_free, 1)
                v.wait_ge(x_free, i + 1)
                nc.vector.bn_stats(stat(i, 0, 6), t[:, 0:512])
                after(nc.vector.bn_stats(stat(i, 6, 12), t[:, 512:D]))
                after(nc.vector.bn_aggr(stat(i, 12, 14), stat(i, 0, 12)))
                nc.vector.tensor_scalar(stat(i, 14, 15), stat(i, 13, 14), EPS, None, ALU.add).then_inc(var_done, 1)
                v.wait_ge(root_done, i + 1)
                after(nc.vector.reciprocal(stat(i, 16, 17), stat(i, 15, 16)))
                after(nc.vector.tensor_scalar(t, t, stat(i, 12, 13), stat(i, 16, 17), ALU.subtract, ALU.mult))
                after(nc.vector.tensor_tensor(t, t, g_row, ALU.mult))
                nc.vector.tensor_tensor(t, t, beta_row, ALU.add).then_inc(normed, 1)
                if i + 2 < tiles:
                    split_y(i + 2)

        @block.tensor
        def _(pe):
            for i in range(tiles):
                pe.wait_ge(y_ready, i + 1)
                if i >= 3:
                    pe.wait_ge(psum_free, i - 2)
                for k in range(KT):
                    if i == 0:
                        pe.wait_ge(w_ready, k + 1)
                    for n, (yt, wt) in enumerate(((m.w_hi, m.h_hi), (m.w_hi, m.h_lo), (m.w_lo, m.h_hi))):
                        for half in range(2):
                            mm = nc.tensor.matmul(m.bank(2 * (i % 3) + half), yt[:, i % 2, k, :],
                                                  wt[:, k, half * 512:half * 512 + 512],
                                                  start=(k == 0 and n == 0), stop=(k == KT - 1 and n == 2))
                mm.then_inc(mm_done, 1)


def backbone(nc, x, ctx, cond, w_mod, b_cols, b_gate, w_in, w_out, ln_g, ln_b, rpb, lam, sub_g, ident, rope, masks, out):
    scratch = lambda n, s: nc.dram_tensor(n, s, F32, kind="Internal").ap()
    x1 = scratch("x1", (TOK, D))
    gate_rows = scratch("gate_rows", (DEPTH, 2, D))
    toeplitz = scratch("toeplitz", (HEADS, GRID_W, RPB_H, GRID_W))
    y_t = [scratch(f"y_t{l}", (D, TOK)) for l in range(DEPTH)]
    rows0 = lambda t: x[t * P:(t + 1) * P, :] if t < LAT_TILES else ctx[(t - LAT_TILES) * P:(t - LAT_TILES + 1) * P, :]
    rows1 = lambda t: x1[t * P:(t + 1) * P, :]
    with ExitStack() as stack:
        m = Memory(nc, stack)
        modulation(nc, m, stack, w_mod, cond, b_cols, lam, sub_g, ident, rpb, toeplitz, gate_rows)
        load_tokens(nc, m, stack, 0, rows0)
        neighbourhood(nc, m, stack, w_in, toeplitz, masks, y_t[0])
        project(nc, m, stack, 0, w_out, y_t[0], gate_rows, b_gate, ln_g, ln_b, rows0, rows1, TOK_TILES)
        load_tokens(nc, m, stack, 1, rows1)
        differential(nc, m, stack, w_in, rope, y_t[1])
        project(nc, m, stack, 1, w_out, y_t[1], gate_rows, b_gate, ln_g, ln_b, rows1,
                lambda t: out[t * P:(t + 1) * P, :], LAT_TILES)


def shape_constants():
    ident = np.eye(P, dtype=np.float32)
    n_freq = HD // 4
    inv = np.float32(10000.0) ** (-np.arange(n_freq, dtype=np.float32) / np.float32(n_freq))
    t = np.arange(SEQ)
    pos = np.stack([t // GRID_W, t % GRID_W]).astype(np.float32)
    dim = np.arange(P) % HD
    ang = pos[dim // 32] * inv[dim % 16].astype(np.float32)[:, None]
    sign = np.where(dim % 32 < 16, -1.0, 1.0).astype(np.float32)[:, None]
    rope = np.stack([np.cos(ang), np.sin(ang) * sign], axis=1).astype(np.float32)
    w = np.arange(P) % GRID_W
    start = np.clip(w - WIN_C // 2, 0, GRID_W - WIN_C)[:, None]
    j = np.arange(GRID_W)[None]
    cols = np.where((j >= start) & (j < start + WIN_C), 0.0, NEG).astype(np.float32)
    every = np.repeat(cols[:, None], SLOTS, axis=1)
    inner = np.repeat(cols[:, None], INNER, axis=1)
    inner[:GRID_W, INNER - 1] = NEG
    inner[GRID_W:, 0] = NEG
    masks = np.concatenate([every.reshape(P, -1), inner.reshape(P, -1)], axis=1)
    return ident, rope, np.ascontiguousarray(masks)


def kernel(x, c, ctx, c_ctx, w_mod, b_mod, w_in, w_out, ln_g, ln_b, na_rpb, diff_lambda, diff_subln_g):
    import concourse.bacc as bacc
    from concourse.bass_utils import run_bass_kernel_spmd

    a = np.ascontiguousarray
    ident, rope, masks = shape_constants()
    cond = a(np.stack([np.asarray(c)[0], np.asarray(c_ctx)]).reshape(2, KT, P).transpose(2, 0, 1))
    b_mod = np.asarray(b_mod)
    b_cols = a(b_mod[:, 0:2 * D].reshape(DEPTH, 2 * KT, P).transpose(2, 0, 1))
    arrays = {
        "x": a(np.asarray(x)[0]), "ctx": a(np.asarray(ctx)[0]), "cond": cond, "w_mod": a(w_mod), "b_cols": b_cols,
        "b_gate": a(b_mod[:, 2 * D:]), "w_in": a(w_in), "w_out": a(w_out), "ln_g": a(ln_g), "ln_b": a(ln_b),
        "rpb": a(np.pad(np.asarray(na_rpb)[0], ((0, 0), (0, 0), (PAD, PAD)))),
        "lam": a(np.asarray(diff_lambda)[0].reshape(-1)), "sub_g": a(np.asarray(diff_subln_g)[0].reshape(P, 1)),
        "ident": ident, "rope": rope, "masks": masks,
    }
    nc = bacc.Bacc("TRN2", target_bir_lowering=False, num_devices=1)
    args = [nc.dram_tensor("in_" + n, v.shape, mybir.dt.from_np(v.dtype), kind="ExternalInput").ap() for n, v in arrays.items()]
    out = nc.dram_tensor("out", (SEQ, D), F32, kind="ExternalOutput").ap()
    backbone(nc, *args, out)
    r = run_bass_kernel_spmd(nc, [{"in_" + n: v for n, v in arrays.items()}], core_ids=[0])
    return r.results[0]["out"].reshape(1, SEQ, D)
```

```python
import math
from contextlib import ExitStack

import concourse.bass as bass
import numpy as np
from concourse import mybir

P = 128
D = 1024
SEQ = 1024
CTX = 256
TOK = SEQ + CTX
KT = D // P
NCH = D // P
LAT_TILES, CTX_TILES = SEQ // P, CTX // P
TOK_TILES = LAT_TILES + CTX_TILES
DEPTH = 2
GRID_W = 64
ROWS = SEQ // GRID_W
WIN_R, WIN_C = 8, 16
HEADS = 16
HD = 64
PAD = 63 - (WIN_C - 1)
RPB_W = 2 * WIN_C - 1 + 2 * PAD
RPB_H = 2 * WIN_R - 1
SLOTS = RPB_H - 1
INNER = WIN_R + 1
EPS = 1e-5
ALPHA = (2.0 * DEPTH) ** 0.25
LAMBDA_INIT = 0.8 - 0.6 * math.exp(-0.3 * 1)
SCALE = HD ** -0.5
NEG = -1e30

F32 = mybir.dt.float32
F32R = mybir.dt.float32r
ALU = mybir.AluOpType
ACT = mybir.ActivationFunctionType
AX = mybir.AxisListType.X

GROUPS = [(0, 512), (512, 512), (1024, 256)]
BLOCKS = [2 * D, D, 0, 3 * D]
SWAP16 = [i ^ 16 for i in range(32)]


CREDIT = 1
ROW_PAD = P
AHEAD = 4


def f(ap):
    return ap.bitcast(F32)


class Memory:

    def __init__(self, nc, stack):
        def sb(name, shape, dt=F32):
            return stack.enter_context(nc.sbuf_tensor(name, shape, dt))

        self.h_hi = sb("h_hi", [P, KT, TOK], F32R)
        self.h_lo = sb("h_lo", [P, KT, TOK], F32R)
        self.w_raw = sb("w_raw", [P, 2, KT, P])
        self.w_hi = sb("w_hi", [P, 2, KT, P], F32R)
        self.w_lo = sb("w_lo", [P, 2, KT, P], F32R)
        self.q_stack = sb("q_stack", [P, 2, TOK], F32R)
        self.k_dup = sb("k_dup", [P, 2, 2, TOK], F32R)
        self.v = sb("v", [P, TOK_TILES, P])
        self.k_raw = sb("k_raw", [P, TOK])
        self.gate = sb("gate", [P, TOK])
        self.y = sb("y", [P, TOK])
        self.big = sb("big", [P, 5120])
        self.aux = sb("aux", [P, 4608])
        self.extra_prob = sb("extra_prob", [P, TOK])
        self.pt = sb("pt", [P, 4, 4 * P])
        self.ident = sb("ident", [P, P])
        self.mean_mat = sb("mean_mat", [P, P])
        self.mod_cols = sb("mod_cols", [P, DEPTH, 2, 2 * KT])
        self.b_cols = sb("b_cols", [P, DEPTH, 2 * KT])
        self.cond = sb("cond", [P, 2, KT])
        self.cond_act = sb("cond_act", [P, 2, KT])
        self.neg_lambda = sb("neg_lambda", [P, 1])
        self.sub_gain = sb("sub_gain", [P, 1])
        self.stats = sb("stats", [P, 96])
        self.pick = sb("pick", [P, 2, 2])
        self.psum = stack.enter_context(nc.psum_tensor("acc", [P, 8, 512], F32))

    def bank(self, b, width=512):
        return self.psum[:, b, 0:width]

    def banks(self, b, first, last):
        return self.psum[:, :, :].rearrange("p b n -> p (b n)")[:, b * 512 + first:b * 512 + last]


def rows_broadcast(ap_row, n):
    return bass.AP(ap_row.tensor, ap_row.offset, [[0, P], [1, n]])


def modulation(nc, m, stack, w_mod, cond_in, b_cols_in, lam_in, sub_in, ident_in, rpb, toeplitz, bands, tile_loads):
    sem = lambda n: stack.enter_context(nc.semaphore("m_" + n))
    slots = [m.w_raw[:, i, :, :].rearrange("p k n -> p (k n)") for i in range(2)] + \
            [b[:, 0:D] for b in (m.k_raw, m.gate, m.y)] + [m.v[:, 0:KT, :].rearrange("p k n -> p (k n)")]
    NS = len(slots)
    PIECES = KT * 2
    small_in, lam_loaded = sem("small_in"), sem("lam_loaded")
    w_in = [sem(f"w_in{s}") for s in range(NS)]
    tanh_done, cond_ready, piece_used = sem("tanh"), sem("cond"), sem("used")
    row_ready, turned, cols_done = sem("row"), sem("turned"), sem("cols")
    dve, lam_exp, const_set = sem("dve"), sem("lam_exp"), sem("const_set")

    row_buf = [m.pt[0:2, i, :] for i in range(4)]
    lam = m.extra_prob[:, 0:4 * HD]
    lam_prod = m.extra_prob[:, 4 * HD:5 * HD]
    sums = m.stats[:, 0:4]

    with nc.Block() as block:
        @block.sync
        def _(sp):
            sp.dma_start(m.cond[:, :, :], cond_in).then_inc(small_in, 16)
            sp.dma_start(m.b_cols[:, :, :], b_cols_in).then_inc(small_in, 16)
            sp.dma_start(m.ident[:, :], ident_in).then_inc(small_in, 16)
            for n in range(PIECES):
                k, j = n // 2, n % 2
                if n >= NS:
                    sp.wait_ge(piece_used, n - NS + 1)
                sp.dma_start(slots[n % NS], w_mod[k * P:(k + 1) * P, j * D:(j + 1) * D]).then_inc(w_in[n % NS], 16)
            tile_loads(sp)

        @block.gpsimd
        def _(pool):
            pool.dma_start(lam, rows_broadcast(lam_in, 4 * HD)).then_inc(lam_loaded, 16)
            pool.dma_start(m.sub_gain[:, :], sub_in).then_inc(lam_loaded, 16)
            for h in range(2):
                expand_band(pool, rpb, toeplitz, h, bands)

        @block.scalar
        def _(act):
            act.wait_ge(small_in, 48)
            nc.scalar.activation(m.cond_act[:, :, :], m.cond[:, :, :], ACT.Tanh, scale=0.5).then_inc(tanh_done, 1)
            act.wait_ge(dve, 2)
            nc.scalar.activation(sums[:, 2:4], sums[:, 0:2], ACT.Exp).then_inc(lam_exp, 1)

        @block.vector
        def _(v):
            v.wait_ge(tanh_done, 1)
            nc.vector.scalar_tensor_tensor(m.cond_act[:, :, :], m.cond_act[:, :, :], 1.0, m.cond[:, :, :],
                                           ALU.add, ALU.mult).then_inc(cond_ready, 1)
            nc.vector.memset(m.mean_mat[:, :], 1.0 / P).then_inc(const_set, 1)
            for r in range(2):
                nc.vector.memset(m.pick[:, r, r:r + 1], 1.0).then_inc(const_set, 1)
                nc.vector.memset(m.pick[:, r, 1 - r:2 - r], 0.0).then_inc(const_set, 1)
            v.wait_ge(lam_loaded, 32)
            for i in range(2):
                if i:
                    v.wait_ge(dve, 1)
                nc.vector.tensor_tensor_reduce(out=lam_prod, in0=lam[:, 2 * i * HD:(2 * i + 1) * HD],
                                               in1=lam[:, (2 * i + 1) * HD:(2 * i + 2) * HD], scale=1.0, scalar=0.0,
                                               op0=ALU.mult, op1=ALU.add, accum_out=sums[:, i:i + 1]).then_inc(dve, 1)
            v.wait_ge(lam_exp, 1)
            nc.vector.tensor_tensor(sums[:, 0:1], sums[:, 3:4], sums[:, 2:3], ALU.subtract).then_inc(dve, 1)
            v.wait_ge(dve, 3)
            nc.vector.tensor_scalar(m.neg_lambda[:, :], sums[:, 0:1], -LAMBDA_INIT, None, ALU.add).then_inc(dve, 1)
            nc.vector.tensor_scalar(m.sub_gain[:, :], m.sub_gain[:, :], 0.5 * (1.0 - LAMBDA_INIT), None, ALU.mult)\
                .then_inc(dve, 1)
            v.wait_ge(piece_used, PIECES)
            for j in range(4):
                nc.vector.tensor_scalar(row_buf[j], m.psum[0:2, j, :], 0.5, None, ALU.mult).then_inc(row_ready, 1)
            v.wait_ge(turned, 1)
            cols = m.bank(6, 64).rearrange("p (k c) -> p c k", c=2)
            for cnd in range(2):
                nc.vector.tensor_tensor(m.mod_cols[:, 0, cnd, :], cols[:, cnd, 0:2 * KT], m.b_cols[:, 0, :], ALU.add)\
                    .then_inc(cols_done, 1)
                v.wait_ge(cols_done, 2 * cnd + 1)
                scale = m.mod_cols[:, 0, cnd, KT:2 * KT]
                nc.vector.tensor_scalar(scale, scale, 1.0, None, ALU.add).then_inc(cols_done, 1)

        @block.tensor
        def _(pe):
            pe.wait_ge(cond_ready, 1)
            for n in range(PIECES):
                k, j = n // 2, n % 2
                pe.wait_ge(w_in[n % NS], 16 * (n // NS + 1))
                for half in range(2):
                    mm = nc.tensor.matmul(m.psum[0:2, 2 * j + half, :], m.cond_act[:, :, k],
                                          slots[n % NS][:, half * 512:(half + 1) * 512],
                                          start=(k == 0), stop=(k == KT - 1))
                mm.then_inc(piece_used, 1)
            pe.wait_ge(row_ready, 4)
            for k in range(2 * KT):
                src = row_buf[k // 4][:, (k % 4) * P:(k % 4 + 1) * P]
                mm = nc.tensor.transpose(m.psum[:, 6, 2 * k:2 * k + 2], src, m.ident[0:2, 0:2])
            mm.then_inc(turned, 1)


def expand_band(pool, rpb, toeplitz, h, bands):
    src = rpb[h, :, 63:127]
    pool.dma_start(toeplitz[h].rearrange("w d j -> d w j"),
                   bass.AP(src.tensor, src.offset, [[RPB_W, RPB_H], [-1, GRID_W], [1, GRID_W]])).then_inc(bands, 16)


class LateModulation:
    AHEAD = 3

    def __init__(self, nc, m, stack, w_mod, mod_rows):
        self.nc, self.m, self.w_mod, self.mod_rows = nc, m, w_mod, mod_rows
        sem = lambda n: stack.enter_context(nc.semaphore("x_" + n))
        self.slots = [m.big[:, 4608:5120], m.extra_prob[:, 0:512], m.extra_prob[:, 512:1024]]
        self.acc = [m.big[:, 3584:4096], m.big[:, 4096:4608]]
        self.row = m.pt[0:2, 3, :]
        self.loaded = [sem(f"loaded{s}") for s in range(3)]
        self.summed, self.reduced, self.row_ready, self.row_stored = sem("summed"), sem("reduced"), sem("row"), sem("stored")
        self.counters = self.loaded + [self.summed, self.reduced, self.row_ready, self.row_stored]
        self.per_slot = [3, 3, 2]

    def load(self, sp, c, u):
        if u >= KT:
            prev = {KT: KT - 2, KT + 1: KT - 1, KT + 2: KT - 3}[u]
        else:
            prev = u - 3
        if prev >= 0:
            sp.wait_ge(self.summed, CREDIT + c * 2 * KT + 2 * (prev + 1))
        k = u % KT
        src = self.w_mod[k * P:(k + 1) * P, bass.ds(c * 512 + (2 * D + u // KT * 512), 512)]
        sp.dma_start(self.slots[k % 3], src).then_inc(self.loaded[k % 3], 16)

    def sum(self, v, c, u):
        v.wait_ge(self.loaded[u % 3], CREDIT + c * 16 * self.per_slot[u % 3] + 16 * (u // 3 + 1))
        if u == 0:
            v.wait_ge(self.reduced, CREDIT + c * 1)
        for cnd in range(2):
            x, coef = self.slots[u % 3], self.m.cond_act[:, cnd, u:u + 1]
            if u == 0:
                ins = self.nc.vector.tensor_scalar(self.acc[cnd], x, coef, None, ALU.mult)
            else:
                if cnd == 0:
                    v.wait_ge(self.summed, CREDIT + c * 2 * KT + 2 * u)
                ins = self.nc.vector.scalar_tensor_tensor(self.acc[cnd], x, coef, self.acc[cnd], ALU.mult, ALU.add)
            ins.then_inc(self.summed, 1)

    def reduce(self, pe, c):
        pe.wait_ge(self.summed, CREDIT + c * 2 * KT + 2 * KT)
        for cnd in range(2):
            mm = self.nc.tensor.matmul(self.m.psum[0:2, 7, :], self.m.pick[:, cnd, :], self.acc[cnd],
                                       start=(cnd == 0), stop=(cnd == 1))
        mm.then_inc(self.reduced, 1)

    def take_row(self, act, c):
        act.wait_ge(self.row_stored, CREDIT + c * 16)
        act.wait_ge(self.reduced, CREDIT + c * 1 + 1)
        self.nc.scalar.activation(self.row, self.m.psum[0:2, 7, :], ACT.Copy, scale=0.5).then_inc(self.row_ready, 1)

    def store_row(self, sp, c):
        sp.wait_ge(self.row_ready, CREDIT + c * 1 + 1)
        sp.dma_start(self.mod_rows[:, bass.ds(c * 512 + ROW_PAD, 512)], self.row).then_inc(self.row_stored, 16)


def token_buffers(m, l):
    wide = lambda t, n: [t[:, i * D:(i + 1) * D] for i in range(n)]
    pt = m.pt[:, :, :].rearrange("p a n -> p (a n)")
    if l == 0:
        return wide(m.big, 5) + wide(m.aux, 4) + wide(pt, 1)
    v = m.v[:, 0:KT, :].rearrange("p k n -> p (k n)")
    return [m.k_raw[:, 0:D], m.gate[:, 0:D], m.y[:, 0:D], v] + wide(pt, 2) + wide(m.big, 4)


EARLY_TILES = [9, 6]
TOKEN_TILES = [range(0, 4), range(4, 8), range(8, 10)]


def send_for_tokens(sp, m, l, rows, loaded, tiles):
    for t in tiles:
        sp.dma_start(token_buffers(m, l)[t], rows(t)).then_inc(loaded[t // 4], 16)


def load_tokens(nc, m, stack, l, p, rows, loaded):
    sem = lambda n: stack.enter_context(nc.semaphore(f"t{l}_" + n))
    turned, modulated, hi_done, lo_done = sem("turned"), sem("modulated"), sem("hi"), sem("lo")
    TILES = TOKEN_TILES
    buf = token_buffers(m, l)
    give_credit(nc, p.counters)
    tmp = [m.extra_prob[:, i * 512:(i + 1) * 512] for i in range(2)]
    steps = [(g, k) for g in range(3) for k in range(KT)]

    with nc.Block() as block:
        @block.sync
        def _(sp):
            send_for_tokens(sp, m, l, rows, loaded, range(EARLY_TILES[l], TOK_TILES))
            p.load(sp, 0, 0)
            p.load(sp, 0, 1)

        @block.tensor
        def _(pe):
            for n, (g, k) in enumerate(steps):
                if k == 0:
                    pe.wait_ge(loaded[g], 16 * len(TILES[g]))
                if n >= 4:
                    pe.wait_ge(modulated, n - 3)
                for i in range(len(TILES[g])):
                    mm = nc.tensor.transpose(m.psum[:, n % 4, i * P:(i + 1) * P], buf[4 * g + i][:, k * P:(k + 1) * P],
                                             m.ident[:, :])
                mm.then_inc(turned, 1)

        @block.scalar
        def _(act):
            for n, (g, k) in enumerate(steps):
                w = GROUPS[g][1]
                cnd = g // 2
                act.wait_ge(turned, n + 1)
                if n >= 2:
                    act.wait_ge(lo_done, n - 1)
                nc.scalar.activation(tmp[n % 2][:, 0:w], m.bank(n % 4, w), ACT.Identity,
                                     scale=m.mod_cols[:, l, cnd, KT + k:KT + k + 1],
                                     bias=m.mod_cols[:, l, cnd, k:k + 1]).then_inc(modulated, 1)

        @block.vector
        def _(v):
            for n, (g, k) in enumerate(steps):
                t0, w = GROUPS[g]
                v.wait_ge(modulated, n + 1)
                nc.vector.tensor_copy(m.h_hi[:, k, t0:t0 + w], tmp[n % 2][:, 0:w]).then_inc(hi_done, 1)
                v.wait_ge(hi_done, n + 1)
                nc.vector.tensor_tensor(m.h_lo[:, k, t0:t0 + w], tmp[n % 2][:, 0:w], f(m.h_hi[:, k, t0:t0 + w]),
                                        ALU.subtract).then_inc(lo_done, 1)


def give_credit(nc, counters):
    with nc.Block() as block:
        @block.sync
        def _(sp):
            for s in counters:
                sp.sem_inc(s, CREDIT)


class Projection:

    def __init__(self, nc, m, stack, l, w_in, rotary):
        self.counters = []

        def sem(n):
            self.counters.append(stack.enter_context(nc.semaphore(f"p{l}_" + n)))
            return self.counters[-1]

        self.nc, self.m, self.w_in, self.l, self.rotary = nc, m, w_in, l, rotary
        self.w_loaded = [sem("w_loaded0"), sem("w_loaded1")]
        self.w_hi, self.w_split, self.proj = sem("w_hi"), sem("w_split"), sem("proj")
        self.evac, self.gate_done = sem("evac"), sem("gate_done")
        self.tanh_done = sem("tanh")
        self.v_turned, self.v_ready = sem("v_turned"), sem("v_ready")
        self.k_own, self.k_ready, self.q_ready = sem("k_own"), sem("k_ready"), sem("q_ready")
        if rotary:
            self.rot_shuffled, self.rot_scaled, self.dve = sem("rot_shuffled"), sem("rot_scaled"), sem("rot_dve")
        self.k_hi, self.q_hi = sem("k_hi"), sem("q_hi")
        lat_only = l == DEPTH - 1
        self.q_groups = 2 if lat_only else 3
        self.q_cols = SEQ if lat_only else TOK
        sizes = [3, 3, self.q_groups, self.q_groups]
        self.cum = [sum(sizes[:b + 1]) for b in range(4)]
        self.G = self.cum[-1]
        self.groups = [(b, g) for b in range(4) for g in range(sizes[b])]
        self.gate_groups = list(range(self.cum[2], self.G))
        self.early_gate = self.gate_groups[:-1]


    def load(self, sp, c, b):
        col = c * P + (BLOCKS[b % 4] + b // 4 * P)
        src = self.w_in[self.l].rearrange("(k p) n -> p k n", p=P)[:, :, bass.ds(col, P)]
        sp.dma_start(self.m.w_raw[:, b % 2, :, :], src).then_inc(self.w_loaded[b % 2], 16)

    def load_second(self, sp):
        for b in (2, 3):
            sp.wait_ge(self.w_split, CREDIT + (b - 1))
            self.load(sp, 0, b)

    def load_next(self, sp, c, blocks=(4, 5, 6, 7)):
        for b in blocks:
            sp.wait_ge(self.w_split, CREDIT + c * 4 + (b - 1))
            self.load(sp, c, b)

    def split_hi_part(self, act, c, b):
        act.wait_ge(self.w_loaded[b % 2], CREDIT + c * 32 + 16 * (b // 2 + 1))
        if b >= 2:
            act.wait_ge(self.proj, CREDIT + c * self.G + ([0] + self.cum)[b - 1])
        self.nc.scalar.activation(self.m.w_hi[:, b % 2, :, :], self.m.w_raw[:, b % 2, :, :], ACT.Copy)\
            .then_inc(self.w_hi, 1)

    def split_lo_part(self, v, c, b):
        v.wait_ge(self.w_hi, CREDIT + c * 4 + (b + 1))
        self.nc.vector.tensor_tensor(self.m.w_lo[:, b % 2, :, :], self.m.w_raw[:, b % 2, :, :],
                                     f(self.m.w_hi[:, b % 2, :, :]), ALU.subtract).then_inc(self.w_split, 1)

    def bank_of(self, j):
        return j % 4 if j < self.cum[2] else 8 - self.G + j

    def product(self, pe, c, j):
        nc, m = self.nc, self.m
        b, g = self.groups[j]
        t0, w = GROUPS[g]
        if g == 0:
            pe.wait_ge(self.w_split, CREDIT + c * 4 + (b + 1))
        if AHEAD <= j < self.cum[2]:
            pe.wait_ge(self.evac, CREDIT + c * self.cum[2] + (j - 3))
        for k in range(KT):
            for i, (wt, ht) in enumerate(((m.w_hi, m.h_hi), (m.w_hi, m.h_lo), (m.w_lo, m.h_hi))):
                mm = nc.tensor.matmul(m.bank(self.bank_of(j), w), wt[:, b % 2, k, :], ht[:, k, t0:t0 + w],
                                      start=(k == 0 and i == 0), stop=(k == KT - 1 and i == 2))
        mm.then_inc(self.proj, 1)

    def turn_v(self, pe, c, g):
        t0, w = GROUPS[g]
        pe.wait_ge(self.evac, CREDIT + c * self.cum[2] + (g + 1))
        if g == 2:
            pe.wait_ge(self.v_ready, CREDIT + c * 3 + 1)
        for i in range(w // P):
            mm = self.nc.tensor.transpose(self.m.psum[:, 4 + g % 2, i * P:(i + 1) * P],
                                          self.m.k_raw[:, t0 + i * P:t0 + (i + 1) * P], self.m.ident[:, :])
        mm.then_inc(self.v_turned, 1)

    def pe_part(self, pe, c, gate_banks_free, extra=lambda e, c: None):
        self.turn_v(pe, c, 0)
        self.turn_v(pe, c, 1)
        self.product(pe, c, AHEAD)
        self.turn_v(pe, c, 2)
        for j in range(AHEAD + 1, self.cum[2]):
            self.product(pe, c, j)
        gate_banks_free(pe)
        extra(pe, c)
        for j in self.early_gate:
            self.product(pe, c, j)
        pe.wait_ge(self.q_ready, CREDIT + (c + 1) * 2 * self.q_groups)
        pe.wait_ge(self.k_ready, CREDIT + c * 2 + 2)

    def late_product(self, pe, c):
        self.product(pe, c, self.G - 1)

    def before_turns(self, pe, c):
        pe.wait_ge(self.gate_done, CREDIT + c * self.q_groups + len(self.early_gate))

    def before_values(self, pe, c):
        pe.wait_ge(self.gate_done, CREDIT + c * self.q_groups + self.q_groups)
        pe.wait_ge(self.v_ready, CREDIT + c * 3 + 3)

    def evacuate(self, act, c, j):
        b, g = self.groups[j]
        t0, w = GROUPS[g]
        dst = (self.m.k_raw, self.m.k_raw, self.m.y)[b]
        act.wait_ge(self.proj, CREDIT + c * self.G + (j + 1))
        if b == 1:
            act.wait_ge(self.v_turned, CREDIT + c * 3 + (g + 1))
        self.nc.scalar.activation(dst[:, t0:t0 + w], self.m.bank(self.bank_of(j), w), ACT.Copy,
                                  scale=SCALE if b == 2 else 1.0).then_inc(self.evac, 1)

    def evacuate_v(self, act, c, g):
        t0, w = GROUPS[g]
        act.wait_ge(self.v_turned, CREDIT + c * 3 + (g + 1))
        self.nc.scalar.activation(self.m.v[:, t0 // P:(t0 + w) // P, :],
                                  self.m.bank(4 + g % 2, w).rearrange("p (t n) -> p t n", n=P), ACT.Copy)\
            .then_inc(self.v_ready, 1)

    def duplicate_k(self, act, c):
        act.wait_ge(self.k_own, CREDIT + c * 2 + 2)
        for h in range(2):
            own, other = slice(64 * h, 64 * h + 64), slice(64 - 64 * h, 128 - 64 * h)
            self.nc.scalar.activation(self.m.k_dup[other, h, :, :], f(self.m.k_dup[own, h, :, :]), ACT.Copy)\
                .then_inc(self.k_ready, 1)

    def gate_tanh(self, act, c, j):
        t0, w = GROUPS[self.groups[j][1]]
        act.wait_ge(self.proj, CREDIT + c * self.G + (j + 1))
        self.nc.scalar.activation(self.m.gate[:, t0:t0 + w], self.m.bank(self.bank_of(j), w), ACT.Tanh, scale=0.5)\
            .then_inc(self.tanh_done, 1)

    def act_part(self, act, c, gate_free, y_free, last, extra=lambda e, c: None):
        self.split_hi_part(act, c, 2)
        self.evacuate_v(act, c, 0)
        self.evacuate(act, c, 3)
        self.evacuate_v(act, c, 1)
        self.evacuate_v(act, c, 2)
        self.evacuate(act, c, 4)
        self.evacuate(act, c, 5)
        self.split_hi_part(act, c, 3)
        y_free(act)
        for j in range(6, self.cum[2]):
            self.evacuate(act, c, j)
        extra(act, c)
        self.duplicate_k(act, c)
        if not last:
            self.split_hi_part(act, c, 4)
        gate_free(act)
        for j in self.early_gate:
            self.gate_tanh(act, c, j)

    def late_tanh(self, act, c):
        self.gate_tanh(act, c, self.G - 1)

    def gate_silu(self, v, c, j):
        g = self.groups[j][1]
        t0, w = GROUPS[g]
        v.wait_ge(self.tanh_done, CREDIT + c * self.q_groups + (g + 1))
        self.nc.vector.scalar_tensor_tensor(self.m.gate[:, t0:t0 + w], self.m.gate[:, t0:t0 + w], 1.0,
                                            self.m.bank(self.bank_of(j), w), ALU.add, ALU.mult)\
            .then_inc(self.gate_done, 1)

    def rotate(self, v, c, x, block, g):
        a, n = GROUPS[g]
        turn = 2 * block + g
        cols = slice(a, a + n)
        rot, scaled = self.m.big[:, cols], self.m.big[:, SEQ + a:SEQ + a + n]
        self.nc.vector.tensor_tensor(scaled, x[:, cols], self.m.aux[:, cols], ALU.mult).then_inc(self.dve, 1)
        self.nc.vector.stream_shuffle(rot, x[:, cols], SWAP16).then_inc(self.rot_shuffled, 1)
        v.wait_ge(self.dve, CREDIT + c * 8 + (2 * turn + 1))
        v.wait_ge(self.rot_scaled, CREDIT + c * 4 + (turn + 1))
        self.nc.vector.tensor_tensor(x[:, cols], scaled, rot, ALU.add).then_inc(self.dve, 1)
        v.wait_ge(self.dve, CREDIT + c * 8 + (2 * turn + 2))

    def scale_partner(self, pool, c):
        for turn in range(4):
            a, n = GROUPS[turn % 2]
            rot, sin = self.m.big[:, a:a + n], self.m.aux[:, SEQ + a:SEQ + a + n]
            pool.wait_ge(self.rot_shuffled, CREDIT + c * 4 + (turn + 1))
            self.nc.gpsimd.tensor_tensor(rot, rot, sin, ALU.mult).then_inc(self.rot_scaled, 1)

    def split_k(self, v, c):
        m = self.m
        for g in range(3):
            if self.rotary and g < 2:
                v.wait_ge(self.evac, CREDIT + c * self.cum[2] + (self.cum[0] + g + 1))
                self.rotate(v, c, m.k_raw, 0, g)
        v.wait_ge(self.evac, CREDIT + c * self.cum[2] + self.cum[1])
        for h in range(2):
            own = slice(64 * h, 64 * h + 64)
            self.nc.vector.tensor_copy(m.k_dup[own, h, 0, :], m.k_raw[own, :]).then_inc(self.k_hi, 1)
        for h in range(2):
            own = slice(64 * h, 64 * h + 64)
            v.wait_ge(self.k_hi, CREDIT + c * 2 + (h + 1))
            self.nc.vector.tensor_tensor(m.k_dup[own, h, 1, :], m.k_raw[own, :], f(m.k_dup[own, h, 0, :]),
                                         ALU.subtract).then_inc(self.k_own, 1)

    def split_q(self, v, c):
        m, n = self.m, self.q_groups
        for g in range(n):
            t0, w = GROUPS[g]
            v.wait_ge(self.evac, CREDIT + c * self.cum[2] + (self.cum[1] + g + 1))
            if self.rotary:
                self.rotate(v, c, m.y, 1, g)
            for h in range(2):
                own = slice(64 * h, 64 * h + 64)
                self.nc.vector.tensor_copy(m.q_stack[own, h, t0:t0 + w], m.y[own, t0:t0 + w]).then_inc(self.q_hi, 1)
            for h in range(2):
                own, other = slice(64 * h, 64 * h + 64), slice(64 - 64 * h, 128 - 64 * h)
                v.wait_ge(self.q_hi, CREDIT + c * 2 * n + (2 * g + h + 1))
                self.nc.vector.tensor_tensor(m.q_stack[other, h, t0:t0 + w], m.y[own, t0:t0 + w],
                                             f(m.q_stack[own, h, t0:t0 + w]), ALU.subtract).then_inc(self.q_ready, 1)

    def dve_part(self, v, c, last, extra=lambda e, c, part: None):
        extra(v, c, 0)
        self.split_lo_part(v, c, 2)
        self.split_k(v, c)
        self.split_lo_part(v, c, 3)
        extra(v, c, 1)
        self.split_q(v, c)
        if not last:
            self.split_lo_part(v, c, 4)
        for j in self.early_gate:
            self.gate_silu(v, c, j)

    def late_silu(self, v, c):
        self.gate_silu(v, c, self.G - 1)


class OutWeights:

    def __init__(self, nc, m, stack, l, w_out):
        self.nc, self.m, self.l, self.w_out = nc, m, l, w_out
        sem = lambda n: stack.enter_context(nc.semaphore(f"w{l}_" + n))
        self.loaded = [sem("loaded0"), sem("loaded1")]
        self.hi, self.ready = sem("hi"), sem("ready")
        self.stage = [m.w_raw[:, s, :, :].rearrange("p k n -> p (k n)") for s in range(2)]

    def load(self, sp, p):
        sp.wait_ge(p.w_split, CREDIT + 4 * NCH)
        for k in range(KT):
            if k >= 2:
                sp.wait_ge(self.ready, k - 1)
            sp.dma_start(self.stage[k % 2], self.w_out[self.l, k * P:(k + 1) * P, :]).then_inc(self.loaded[k % 2], 16)

    def split_hi(self, act, p, k):
        if k == 0:
            act.wait_ge(p.proj, CREDIT + NCH * p.G)
        act.wait_ge(self.loaded[k % 2], 16 * (k // 2 + 1))
        self.nc.scalar.activation(self.m.h_hi[:, k, 0:D], self.stage[k % 2], ACT.Copy).then_inc(self.hi, 1)

    def split_lo(self, v, k):
        v.wait_ge(self.hi, k + 1)
        self.nc.vector.tensor_tensor(self.m.h_lo[:, k, 0:D], self.stage[k % 2], f(self.m.h_hi[:, k, 0:D]),
                                     ALU.subtract).then_inc(self.ready, 1)


def each_chunk(engine, chunk):
    with engine.Fori(0, NCH - 1) as c:
        chunk(c, False)
    chunk(NCH - 1, True)


class Item:

    def __init__(self, head, qt):
        self.head, self.qt = head, qt
        self.local = qt < LAT_TILES
        self.rows = 0
        if self.local:
            r = 2 * qt
            start = [min(max(x - WIN_R // 2, 0), ROWS - WIN_R) for x in (r, r + 1)]
            self.k0 = start[0]
            self.rows = start[1] + WIN_R - start[0]
            self.slot = self.k0 - r + WIN_R - 2
        self.width = CTX + self.rows * GRID_W
        tiles = [LAT_TILES + i for i in range(CTX_TILES)]
        if self.local:
            tiles += [self.k0 // 2 + i for i in range((self.rows + 1) // 2)]
        self.key_tiles = tiles
        self.y_group = head * 3 + qt // 4


def neighbourhood(nc, m, stack, p, out_w, rpb, toeplitz, bands, masks_in, w_mod, mod_rows, y_out):
    l = 0
    counters = []

    def sem(n):
        counters.append(stack.enter_context(nc.semaphore("n_" + n)))
        return counters[-1]

    masks_loaded = stack.enter_context(nc.semaphore("n_masks"))
    bias_loaded, bias_ready, bias_tmp = sem("bias_loaded"), sem("bias_ready"), sem("bias_tmp")
    s_done, raw_max, max_done = sem("s_done"), sem("raw_max"), sem("max_done")
    exp_done, recip_done, p_ready = sem("exp_done"), sem("recip"), sem("p_ready")
    turned, pt_ready, av_done, y_ready, y_stored = sem("turned"), sem("pt_ready"), sem("av_done"), sem("y_ready"), sem("y_stored")
    pad_set = stack.enter_context(nc.semaphore("n_pad"))
    late = LateModulation(nc, m, stack, w_mod, mod_rows)
    counters += late.counters

    items = [Item(h, qt) for h in range(2) for qt in range(TOK_TILES)]
    NI = len(items)
    NL = sum(it.local for it in items)
    WMAX = CTX + (INNER + 1) * GRID_W
    PB = 4
    prob = m.big[:, 0:PB * WMAX].rearrange("p (b n) -> p b n", b=PB)
    mask_w = SLOTS * GRID_W
    inner_w = INNER * GRID_W
    mask = m.aux[:, 0:mask_w + inner_w]
    mask_all, mask_inner = mask[:, 0:mask_w], mask[:, mask_w:]
    bias = m.aux[:, 1536:1536 + 2 * mask_w].rearrange("p (h n) -> p h n", h=2)
    bias_inner = m.aux[:, 1536 + 2 * mask_w:1536 + 2 * (mask_w + inner_w)].rearrange("p (h n) -> p h n", h=2)
    turns = [(i, a, min(4, len(it.key_tiles) - a)) for i, it in enumerate(items) for a in range(0, len(it.key_tiles), 4)]
    of_item = [[n for n, t in enumerate(turns) if t[0] == i] for i in range(NI)]
    NT = len(turns)
    YG = 6
    last_item = [max(i for i, it in enumerate(items) if it.y_group == g) for g in range(YG)]
    local_before = [sum(x.local for x in items[:i]) for i in range(NI + 1)]
    give_credit(nc, counters)
    assert NI % 2 == 0 and NT % 6 == 0 and NI % PB == 0

    def stat(i, col):
        return m.stats[:, (i % 4) * 8 + col:(i % 4) * 8 + col + 1]

    with nc.Block() as block:
        @block.sync
        def _(sp):
            sp.dma_start(mask, masks_in).then_inc(masks_loaded, 16)

            def load_bias(c):
                for half in range(2):
                    src = toeplitz[bass.ds(c * 2, 2), :, 1 - half:1 - half + SLOTS, :].rearrange("h w d j -> w h (d j)")
                    sp.dma_start(bias[64 * half:64 * half + 64, :, :], src).then_inc(bias_loaded, 16)

            def chunk(c, last):
                late.load(sp, c, 3)
                late.load(sp, c, 4)
                late.load(sp, c, 5)
                if not last:
                    p.load_next(sp, c, (4,))
                late.load(sp, c, 6)
                late.load(sp, c, 7)
                late.store_row(sp, c)
                if not last:
                    p.load_next(sp, c, (5, 6, 7))
                    for u in range(KT, KT + late.AHEAD):
                        late.load(sp, c, u)
                    sp.wait_ge(max_done, CREDIT + c * NI + NI)
                    load_bias(c + 1)
                else:
                    out_w.load(sp, p)
                sp.wait_ge(y_ready, CREDIT + c * YG + YG)
                sp.dma_start(y_out[bass.ds(c * P, P), :], m.y[:, :]).then_inc(y_stored, 16)

            sp.wait_ge(bands, 32)
            load_bias(0)
            p.load_second(sp)
            for u in range(late.AHEAD):
                late.load(sp, 0, u)
            sp.wait_ge(bands, 16 * HEADS)
            each_chunk(sp, chunk)
            sp.wait_ge(late.row_stored, CREDIT + 16 * NCH)
            sp.wait_ge(y_stored, CREDIT + 16 * NCH)

        @block.gpsimd
        def _(pool):
            nc.gpsimd.memset(prob[:, :, WMAX - GRID_W:WMAX], 0.0).then_inc(pad_set, 1)
            for h in range(2, HEADS):
                expand_band(pool, rpb, toeplitz, h, bands)
            pool.wait_ge(masks_loaded, 16)
            with pool.Fori(0, NCH) as c:
                pool.wait_ge(bias_loaded, CREDIT + c * 32 + 32)
                for h in range(2):
                    nc.gpsimd.tensor_tensor(bias_inner[:, h, :], bias[:, h, 2 * GRID_W:2 * GRID_W + inner_w], mask_inner,
                                            ALU.add).then_inc(bias_tmp, 1)
                for h in range(2):
                    pool.wait_ge(bias_tmp, CREDIT + c * 2 + (h + 1))
                    nc.gpsimd.tensor_tensor(bias[:, h, :], bias[:, h, :], mask_all, ALU.add).then_inc(bias_ready, 1)

        @block.scalar
        def _(act):
            p.split_hi_part(act, 0, 0)
            p.split_hi_part(act, 0, 1)
            for j in range(3):
                p.evacuate(act, 0, j)
            act.wait_ge(pad_set, 1)

            def chunk(c, last):
                def exp(i):
                    it = items[i]
                    act.wait_ge(max_done, CREDIT + c * NI + (i + 1))
                    nc.scalar.activation(prob[:, i % PB, 0:it.width], m.banks(2 * (i % 2), 0, it.width), ACT.Exp,
                                         bias=stat(i, 2), accum_out=stat(i, 3)).then_inc(exp_done, 1)

                def evac(n):
                    w = turns[n][2] * P
                    act.wait_ge(turned, CREDIT + c * NT + (n + 1))
                    act.wait_ge(av_done, CREDIT + c * NT + max(n - 2, 0))
                    nc.scalar.activation(m.pt[:, n % 3, 0:w], m.bank(4 + n % 2, w), ACT.Copy).then_inc(pt_ready, 1)

                p.act_part(act, c, lambda e: e.wait_ge(y_ready, CREDIT + c * YG), lambda e: e.wait_ge(y_stored, CREDIT + c * 16),
                           last, late.take_row)
                exp(0)
                p.late_tanh(act, c)
                for i in range(NI):
                    if i + 1 < NI:
                        exp(i + 1)
                    for n in of_item[i]:
                        evac(n)
                    if i == NI // 2 and not last:
                        p.split_hi_part(act, c, 5)
                    if i % 2 and 3 <= i < 3 + 2 * KT and last:
                        out_w.split_hi(act, p, i // 2 - 1)
                if not last:
                    for j in range(3):
                        p.evacuate(act, c + 1, j)

            each_chunk(act, chunk)

        @block.vector
        def _(v):
            p.split_lo_part(v, 0, 0)
            p.split_lo_part(v, 0, 1)

            def chunk(c, last):
                def row_max(i):
                    it = items[i]
                    s = 2 * (i % 2)
                    v.wait_ge(s_done, CREDIT + c * NI + (i + 1))
                    if not it.local:
                        nc.vector.reduce_max(stat(i, 2), m.banks(s, 0, CTX), AX, negate=True).then_inc(max_done, 1)
                        return
                    nl = local_before[i]
                    nc.vector.reduce_max(stat(i, 0), m.banks(s, 0, CTX), AX)
                    if it.rows == INNER:
                        b = bias_inner[:, it.head, :]
                    else:
                        b = bias[:, it.head, it.slot * GRID_W:(it.slot + WIN_R) * GRID_W]
                    loc = m.banks(s, CTX, it.width)
                    nc.vector.tensor_tensor_reduce(out=loc, in0=loc, in1=b, scale=1.0, scalar=-3e38, op0=ALU.add,
                                                   op1=ALU.max, accum_out=stat(i, 1)).then_inc(raw_max, 1)
                    v.wait_ge(raw_max, CREDIT + c * NL + (nl + 1))
                    nc.vector.reduce_max(stat(i, 2), m.stats[:, (i % 4) * 8:(i % 4) * 8 + 2], AX, negate=True)\
                        .then_inc(max_done, 1)

                def normalise(i):
                    it = items[i]
                    v.wait_ge(exp_done, CREDIT + c * NI + (i + 1))
                    nc.vector.reciprocal(stat(i, 4), stat(i, 3)).then_inc(recip_done, 1)
                    v.wait_ge(recip_done, CREDIT + c * NI + (i + 1))
                    pr = prob[:, i % PB, 0:it.width]
                    nc.vector.tensor_scalar(pr, pr, stat(i, 4), None, ALU.mult).then_inc(p_ready, 1)

                def gate_y(g):
                    h, t0 = g // 3, (g % 3) * 512
                    w = min(512, TOK - t0)
                    own = slice(64 * h, 64 * h + 64)
                    v.wait_ge(av_done, CREDIT + c * NT + (of_item[last_item[g]][-1] + 1))
                    nc.vector.scalar_tensor_tensor(m.y[own, t0:t0 + w], m.psum[own, 6 + g % 2, 0:w], 0.5,
                                                   m.gate[own, t0:t0 + w], ALU.mult, ALU.mult).then_inc(y_ready, 1)

                def late_sums(v, c, part):
                    for u in range(KT)[part * late.AHEAD:][:late.AHEAD if part == 0 else None]:
                        late.sum(v, c, u)

                p.dve_part(v, c, last, late_sums)
                v.wait_ge(bias_ready, CREDIT + c * 2 + 2)
                row_max(0)
                row_max(1)
                p.late_silu(v, c)
                for i in range(NI):
                    normalise(i)
                    if i + 2 < NI:
                        row_max(i + 2)
                    if i - 2 in last_item:
                        gate_y(last_item.index(i - 2))
                    if i == NI // 2 and not last:
                        p.split_lo_part(v, c, 5)
                    if i % 2 == 0 and 4 <= i < 4 + 2 * KT and last:
                        out_w.split_lo(v, i // 2 - 2)
                for g in range(YG):
                    if last_item[g] + 2 >= NI:
                        gate_y(g)

            each_chunk(v, chunk)

        @block.tensor
        def _(pe):
            for j in range(AHEAD):
                p.product(pe, 0, j)

            def chunk(c, last):
                def scores(i):
                    it = items[i]
                    s = 2 * (i % 2)
                    if i >= 2:
                        pe.wait_ge(exp_done, CREDIT + c * NI + (i - 1))
                    parts = [(s, 0, CTX, SEQ)]
                    if it.local:
                        k0 = it.k0 * GRID_W
                        parts += [(s, CTX, 256, k0), (s + 1, 0, (it.rows - 4) * GRID_W, k0 + 256)]
                    for b, col, w, key in parts:
                        for part in range(2):
                            mm = nc.tensor.matmul(m.psum[:, b, col:col + w], m.q_stack[:, it.head, it.qt * P:(it.qt + 1) * P],
                                                  m.k_dup[:, it.head, part, key:key + w], start=(part == 0), stop=(part == 1))
                    mm.then_inc(s_done, 1)

                def turn(n):
                    i, a, cnt = turns[n]
                    pe.wait_ge(p_ready, CREDIT + c * NI + (i + 1))
                    if n >= 2:
                        pe.wait_ge(pt_ready, CREDIT + c * NT + (n - 1))
                    for t in range(cnt):
                        mm = nc.tensor.transpose(m.psum[:, 4 + n % 2, t * P:(t + 1) * P],
                                                 prob[:, i % PB, (a + t) * P:(a + t + 1) * P], m.ident[:, :])
                    mm.then_inc(turned, 1)

                def values(n):
                    i, a, cnt = turns[n]
                    it = items[i]
                    if n == 0:
                        p.before_values(pe, c)
                    pe.wait_ge(pt_ready, CREDIT + c * NT + (n + 1))
                    if a == 0 and it.qt % 4 == 0:
                        pe.wait_ge(y_ready, CREDIT + c * YG + max(it.y_group - 1, 0))
                    for t in range(cnt):
                        mm = nc.tensor.matmul(m.psum[:, 6 + it.y_group % 2, (it.qt % 4) * P:(it.qt % 4 + 1) * P],
                                              m.v[:, it.key_tiles[a + t], :], m.pt[:, n % 3, t * P:(t + 1) * P],
                                              start=(a + t == 0), stop=(a + t == len(it.key_tiles) - 1))
                    mm.then_inc(av_done, 1)

                def ahead(j):
                    if not last:
                        pe.wait_ge(exp_done, CREDIT + c * NI + (NI - 1 if j < 2 else NI))
                        p.product(pe, c + 1, j)

                p.pe_part(pe, c, lambda e: e.wait_ge(y_ready, CREDIT + c * YG), late.reduce)
                scores(0)
                scores(1)
                pe.wait_ge(late.row_ready, CREDIT + c * 1 + 1)
                p.late_product(pe, c)
                p.before_turns(pe, c)
                for i in range(NI + 1):
                    if i + 2 < NI:
                        scores(i + 2)
                    else:
                        ahead(i + 2 - NI)
                    new = of_item[i] if i < NI else []
                    old = of_item[i - 1] if i else []
                    for n in range(2):
                        if n < len(new):
                            turn(new[n])
                        if n < len(old):
                            values(old[n])
                ahead(3)

            each_chunk(pe, chunk)


def differential(nc, m, stack, p, out_w, rope_in, y_out):
    l = 1
    counters = []

    def sem(n):
        counters.append(stack.enter_context(nc.semaphore("d_" + n)))
        return counters[-1]

    rope_loaded = stack.enter_context(nc.semaphore("d_rope"))
    s_done, max_done, exp_done, coef, p_ready = sem("s_done"), sem("max_done"), sem("exp_done"), sem("coef"), sem("p_ready")
    turned, pt_ready, av_done = sem("turned"), sem("pt_ready"), sem("av_done")
    y_raw, sq_done, ms_done, var_done = sem("y_raw"), sem("sq_done"), sem("ms_done"), sem("var_done")
    root_done, inv_done, diag_ready, spread = sem("root_done"), sem("inv_done"), sem("diag_ready"), sem("spread")
    y_ready, y_stored, fin = sem("y_ready"), sem("y_stored"), sem("fin")

    NQ = LAT_TILES
    KEYS = TOK_TILES
    turns = [(t, a, min(4, KEYS - a)) for t in range(NQ) for a in range(0, KEYS, 4)]
    TPT = 3
    NT = len(turns)
    bufs = [m.big[:, i * TOK:(i + 1) * TOK] for i in range(4)] + [m.extra_prob[:, :]]
    prob = lambda mp, t: bufs[t % 3] if mp == 0 else bufs[3 + t % 2]
    y_sb, sq = m.aux[:, 2048:3072], m.aux[:, 3072:4096]
    stat = lambda t, col: m.stats[:, (t % 2) * 8 + col:(t % 2) * 8 + col + 1]
    eps_col = lambda t: m.stats[:, 32 + t:33 + t]
    give_credit(nc, counters)
    variances, roots, inv_rms = (m.stats[:, 40 + i * NQ:40 + (i + 1) * NQ] for i in range(3))

    with nc.Block() as block:
        @block.sync
        def _(sp):
            sp.dma_start(m.aux[:, 0:2 * SEQ].rearrange("p (a n) -> p a n", a=2), rope_in).then_inc(rope_loaded, 16)
            p.load_second(sp)

            def chunk(c, last):
                if not last:
                    p.load_next(sp, c)
                else:
                    out_w.load(sp, p)
                sp.wait_ge(y_ready, CREDIT + c * 2 + 2)
                sp.dma_start(y_out[bass.ds(c * P, P), 0:SEQ], m.y[:, 0:SEQ]).then_inc(y_stored, 16)

            each_chunk(sp, chunk)
            sp.wait_ge(y_stored, CREDIT + 16 * NCH)

        @block.gpsimd
        def _(pool):
            pool.wait_ge(rope_loaded, 16)
            with pool.Fori(0, NCH) as c:
                p.scale_partner(pool, c)

        @block.scalar
        def _(act):
            p.split_hi_part(act, 0, 0)
            p.split_hi_part(act, 0, 1)
            for j in range(3):
                p.evacuate(act, 0, j)

            def chunk(c, last):
                def exp(mp, t):
                    act.wait_ge(max_done, CREDIT + c * 2 * NQ + (2 * t + mp + 1))
                    nc.scalar.activation(prob(mp, t), m.banks(3 * mp, 0, TOK), ACT.Exp,
                                         bias=stat(t, mp), accum_out=stat(t, 2 + mp)).then_inc(exp_done, 1)

                def evac(n):
                    w = turns[n][2] * P
                    act.wait_ge(turned, CREDIT + c * NT + (n + 1))
                    act.wait_ge(av_done, CREDIT + c * NT + max(n - 3, 0))
                    nc.scalar.activation(m.pt[:, n % 4, 0:w], m.bank(6, w), ACT.Copy).then_inc(pt_ready, 1)

                def take_y(half):
                    cols = slice(half * 512, half * 512 + 512)
                    act.wait_ge(av_done, CREDIT + c * NT + 4 * TPT * (half + 1))
                    nc.scalar.activation(y_sb[:, cols], m.bank(7), ACT.Copy).then_inc(y_raw, 1)
                    act.wait_ge(y_raw, CREDIT + c * 2 + (half + 1))
                    nc.scalar.activation(sq[:, cols], y_sb[:, cols], ACT.Square).then_inc(sq_done, 1)

                p.act_part(act, c, lambda e: e.wait_ge(y_ready, CREDIT + c * 2), lambda e: e.wait_ge(y_stored, CREDIT + c * 16),
                           last)
                exp(0, 0)
                exp(1, 0)
                p.late_tanh(act, c)
                exp(0, 1)
                evac(0)
                exp(1, 1)
                for t in range(NQ):
                    if t == 4:
                        take_y(0)
                    evac(TPT * t + 1)
                    if t + 2 < NQ:
                        exp(0, t + 2)
                    evac(TPT * t + 2)
                    if t + 1 < NQ:
                        evac(TPT * t + 3)
                    if t + 2 < NQ:
                        exp(1, t + 2)
                    if t == 3 and not last:
                        p.split_hi_part(act, c, 5)
                    if last:
                        out_w.split_hi(act, p, t)
                take_y(1)
                if not last:
                    for j in range(3):
                        p.evacuate(act, c + 1, j)
                act.wait_ge(var_done, CREDIT + c * 1 + 1)
                nc.scalar.activation(roots, variances, ACT.Sqrt).then_inc(root_done, 1)

            each_chunk(act, chunk)

        @block.vector
        def _(v):
            p.split_lo_part(v, 0, 0)
            p.split_lo_part(v, 0, 1)
            v.wait_ge(rope_loaded, 16)

            def chunk(c, last):
                def row_max(mp, t):
                    v.wait_ge(s_done, CREDIT + c * 2 * NQ + (2 * t + mp + 1))
                    nc.vector.reduce_max(stat(t, mp), m.banks(3 * mp, 0, TOK), AX, negate=True).then_inc(max_done, 1)

                def combine(t):
                    v.wait_ge(exp_done, CREDIT + c * 2 * NQ + (2 * t + 2))
                    nc.vector.reciprocal(stat(t, 4), stat(t, 3)).then_inc(coef, 1)
                    nc.vector.tensor_scalar(eps_col(t), stat(t, 2), stat(t, 2), EPS, ALU.mult, ALU.mult).then_inc(coef, 1)
                    v.wait_ge(coef, CREDIT + c * 3 * NQ + (3 * t + 2))
                    nc.vector.tensor_scalar(stat(t, 5), stat(t, 2), stat(t, 4), m.neg_lambda[:, :], ALU.mult, ALU.mult)\
                        .then_inc(coef, 1)
                    v.wait_ge(coef, CREDIT + c * 3 * NQ + (3 * t + 3))
                    e0, e1 = prob(0, t), prob(1, t)
                    nc.vector.scalar_tensor_tensor(e0, e1, stat(t, 5), e0, ALU.mult, ALU.add).then_inc(p_ready, 1)

                def root_mean_square():
                    v.wait_ge(ms_done, CREDIT + c * NQ + NQ)
                    nc.vector.tensor_tensor(variances, m.bank(6, NQ), m.stats[:, 32:32 + NQ], ALU.add).then_inc(var_done, 1)
                    v.wait_ge(root_done, CREDIT + c * 1 + 1)
                    nc.vector.reciprocal(inv_rms, roots).then_inc(inv_done, 1)
                    v.wait_ge(inv_done, CREDIT + c * 1 + 1)
                    for t in range(NQ):
                        nc.vector.tensor_scalar(sq[:, t * P:(t + 1) * P], m.ident[:, :], inv_rms[:, t:t + 1], float(P),
                                                ALU.mult, ALU.mult).then_inc(diag_ready, 1)

                def finish(half):
                    cols = slice(half * 512, half * 512 + 512)
                    v.wait_ge(spread, CREDIT + c * 2 + (half + 1))
                    nc.vector.scalar_tensor_tensor(y_sb[:, cols], y_sb[:, cols], m.sub_gain[:, :], m.bank(6 + half),
                                                   ALU.mult, ALU.mult).then_inc(fin, 1)
                    v.wait_ge(fin, CREDIT + c * 2 + (half + 1))
                    nc.vector.tensor_tensor(m.y[:, cols], y_sb[:, cols], m.gate[:, cols], ALU.mult).then_inc(y_ready, 1)

                p.dve_part(v, c, last)
                row_max(0, 0)
                row_max(1, 0)
                combine(0)
                for t in range(NQ):
                    if t + 1 < NQ:
                        row_max(0, t + 1)
                    if t == 0:
                        p.late_silu(v, c)
                    if t:
                        combine(t)
                    if t + 1 < NQ:
                        row_max(1, t + 1)
                    if t == 4 and not last:
                        p.split_lo_part(v, c, 5)
                    if last and t:
                        out_w.split_lo(v, t - 1)
                if last:
                    out_w.split_lo(v, KT - 1)
                root_mean_square()
                finish(0)
                finish(1)

            each_chunk(v, chunk)

        @block.tensor
        def _(pe):
            for j in range(AHEAD):
                p.product(pe, 0, j)

            def chunk(c, last):
                def scores(mp, t):
                    if t:
                        pe.wait_ge(exp_done, CREDIT + c * 2 * NQ + (2 * (t - 1) + mp + 1))
                    for g, (k0, w) in enumerate(GROUPS):
                        for part in range(2):
                            mm = nc.tensor.matmul(m.bank(3 * mp + g, w), m.q_stack[:, mp, t * P:(t + 1) * P],
                                                  m.k_dup[:, mp, part, k0:k0 + w], start=(part == 0), stop=(part == 1))
                    mm.then_inc(s_done, 1)

                def turn(n):
                    t, a, cnt = turns[n]
                    pe.wait_ge(p_ready, CREDIT + c * NQ + (t + 1))
                    pe.wait_ge(pt_ready, CREDIT + c * NT + n)
                    for i in range(cnt):
                        mm = nc.tensor.transpose(m.psum[:, 6, i * P:(i + 1) * P],
                                                 prob(0, t)[:, (a + i) * P:(a + i + 1) * P], m.ident[:, :])
                    mm.then_inc(turned, 1)

                def values(n):
                    t, a, cnt = turns[n]
                    if n == 0:
                        p.before_values(pe, c)
                    pe.wait_ge(pt_ready, CREDIT + c * NT + (n + 1))
                    if a == 0 and t % 4 == 0:
                        pe.wait_ge(y_raw, CREDIT + c * 2 + t // 4)
                    for i in range(cnt):
                        mm = nc.tensor.matmul(m.psum[:, 7, (t % 4) * P:(t % 4 + 1) * P], m.v[:, a + i, :],
                                              m.pt[:, n % 4, i * P:(i + 1) * P], start=(a + i == 0), stop=(a + i == KEYS - 1))
                    mm.then_inc(av_done, 1)

                def ahead(j):
                    if not last:
                        pe.wait_ge(exp_done, CREDIT + c * 2 * NQ + (2 * NQ - 1 if j < 3 else 2 * NQ))
                        p.product(pe, c + 1, j)

                p.pe_part(pe, c, lambda e: e.wait_ge(y_ready, CREDIT + c * 2))
                scores(0, 0)
                scores(1, 0)
                p.late_product(pe, c)
                scores(0, 1)
                scores(1, 1)
                p.before_turns(pe, c)
                for t in range(NQ):
                    turn(TPT * t)
                    if t + 2 < NQ:
                        scores(0, t + 2)
                    else:
                        ahead(t + 2 - NQ)
                    if t:
                        values(TPT * t - 1)
                    turn(TPT * t + 1)
                    if t + 2 < NQ:
                        scores(1, t + 2)
                    values(TPT * t)
                    turn(TPT * t + 2)
                    values(TPT * t + 1)
                values(NT - 1)
                ahead(2)
                pe.wait_ge(sq_done, CREDIT + c * 2 + 2)
                for t in range(NQ):
                    nc.tensor.matmul(m.psum[:, 6, t:t + 1], sq[:, t * P:(t + 1) * P], m.mean_mat[:, 0:1],
                                     start=True, stop=True).then_inc(ms_done, 1)
                ahead(3)
                for half in range(2):
                    pe.wait_ge(diag_ready, CREDIT + c * NQ + 4 * (half + 1))
                    nc.tensor.matmul(m.bank(6 + half), m.mean_mat[:, :], sq[:, half * 512:half * 512 + 512],
                                     start=True, stop=True).then_inc(spread, 1)

            each_chunk(pe, chunk)


def project(nc, m, stack, l, out_w, y_in, gate_of, mod_rows, b_gate, ln_g, ln_b, rows, out_rows, tiles,
            after_store=lambda sp, stored: None):
    sem = lambda n: stack.enter_context(nc.semaphore(f"o{l}_" + n))
    y_loaded, x_loaded = ([sem(f"{n}{s}") for s in range(2)] for n in ("y", "x"))
    stored = [sem(f"stored{s}") for s in range(2)]
    y_hi, y_ready, mm_done = sem("y_hi"), sem("y_ready"), sem("mm_done")
    rows_in, gains, dve, psum_free, x_free = sem("rows_in"), sem("gains"), sem("dve"), sem("psum_free"), sem("x_free")
    var_done, root_done, normed = sem("var"), sem("root"), sem("normed")
    if l == 0:
        cols_in, cols_turned, cols_done = sem("cols_in"), sem("cols_turned"), sem("cols_done")

    x_buf = [m.big[:, s * D:(s + 1) * D] for s in range(2)]
    t_buf = [m.big[:, (2 + s) * D:(3 + s) * D] for s in range(2)]
    b_row = m.big[:, 4 * D:5 * D]
    gain = [m.aux[:, s * D:(s + 1) * D] for s in range(2)]
    g_row, beta_row = m.aux[:, 2 * D:3 * D], m.aux[:, 3 * D:4 * D]
    conds = 2 if tiles > LAT_TILES else 1

    def stat(i, a, b):
        return m.stats[:, (i % 2) * 24 + a:(i % 2) * 24 + b]

    def send_for_y(queue, i):
        queue.dma_start(m.w_raw[:, i % 2, :, :], y_in.rearrange("(k p) n -> p k n", p=P)[:, :, i * P:(i + 1) * P])\
            .then_inc(y_loaded[i % 2], 16)

    with nc.Block() as block:
        @block.sync
        def _(sp):
            sp.wait_ge(y_loaded[0], 16)
            for cnd in range(conds):
                sp.dma_start(gain[cnd], rows_broadcast(gate_of(cnd), D)).then_inc(rows_in, 16)
            sp.dma_start(b_row, rows_broadcast(b_gate[l, :], D)).then_inc(rows_in, 16)
            sp.dma_start(g_row, rows_broadcast(ln_g[l, :], D)).then_inc(rows_in, 16)
            sp.dma_start(beta_row, rows_broadcast(ln_b[l, :], D)).then_inc(rows_in, 16)
            if l == 0:
                for cnd in range(2):
                    sp.dma_start(m.v[2 * KT * cnd:2 * KT * (cnd + 1), KT, :],
                                 mod_rows[cnd, ROW_PAD + D:ROW_PAD + 3 * D].rearrange("(k p) -> k p", p=P)).then_inc(cols_in, 16)
            after_store(sp, stored)

        @block.gpsimd
        def _(pool):
            for i in range(tiles):
                if i >= 2:
                    pool.wait_ge(y_ready, i - 1)
                send_for_y(pool, i)
                if i >= 2:
                    pool.wait_ge(x_free, i - 1)
                pool.dma_start(x_buf[i % 2], rows(i)).then_inc(x_loaded[i % 2], 16)

        @block.scalar
        def _(act):
            def split_y(i):
                act.wait_ge(y_loaded[i % 2], 16 * (i // 2 + 1))
                if i >= 2:
                    act.wait_ge(mm_done, i - 1)
                nc.scalar.activation(m.w_hi[:, i % 2, :, :], m.w_raw[:, i % 2, :, :], ACT.Copy).then_inc(y_hi, 1)

            split_y(0)
            split_y(1)
            for i in range(tiles):
                act.wait_ge(var_done, i + 1)
                nc.scalar.activation(stat(i, 15, 16), stat(i, 14, 15), ACT.Sqrt).then_inc(root_done, 1)
                act.wait_ge(normed, i + 1)
                act.dma_start(out_rows(i), t_buf[i % 2]).then_inc(stored[i % 2], 16)
                if i + 2 < tiles:
                    split_y(i + 2)
            for s in range(2):
                act.wait_ge(stored[s], 16 * (tiles // 2))

        @block.vector
        def _(v):
            count = [0]

            def after(ins):
                count[0] += 1
                ins.then_inc(dve, 1)
                v.wait_ge(dve, count[0])

            def split_y(i):
                v.wait_ge(y_hi, i + 1)
                nc.vector.tensor_tensor(m.w_lo[:, i % 2, :, :], m.w_raw[:, i % 2, :, :], f(m.w_hi[:, i % 2, :, :]),
                                        ALU.subtract).then_inc(y_ready, 1)

            split_y(0)
            split_y(1)
            v.wait_ge(rows_in, 16 * (3 + conds))
            for cnd in range(conds):
                nc.vector.scalar_tensor_tensor(gain[cnd], gain[cnd], 1.0, b_row, ALU.add, ALU.add).then_inc(gains, 1)
            if l == 0:
                v.wait_ge(cols_turned, 1)
                for cnd in range(2):
                    cols = m.mod_cols[:, 1, cnd, :]
                    nc.vector.tensor_tensor(cols, m.psum[:, 6, 2 * KT * cnd:2 * KT * (cnd + 1)], m.b_cols[:, 1, :], ALU.add).then_inc(cols_done, 1)
                    v.wait_ge(cols_done, 2 * cnd + 1)
                    nc.vector.tensor_scalar(cols[:, KT:], cols[:, KT:], 1.0, None, ALU.add).then_inc(cols_done, 1)
            v.wait_ge(gains, conds)
            for i in range(tiles):
                t, x = t_buf[i % 2], x_buf[i % 2]
                b = 2 * (i % 3)
                v.wait_ge(mm_done, i + 1)
                if i >= 2:
                    v.wait_ge(stored[i % 2], 16 * (i // 2))
                nc.vector.tensor_tensor(t, m.banks(b, 0, D), gain[i // LAT_TILES], ALU.mult).then_inc(psum_free, 1)
                v.wait_ge(psum_free, i + 1)
                v.wait_ge(x_loaded[i % 2], 16 * (i // 2 + 1))
                nc.vector.scalar_tensor_tensor(t, x, ALPHA, t, ALU.mult, ALU.add).then_inc(x_free, 1)
                v.wait_ge(x_free, i + 1)
                nc.vector.bn_stats(stat(i, 0, 6), t[:, 0:512])
                after(nc.vector.bn_stats(stat(i, 6, 12), t[:, 512:D]))
                after(nc.vector.bn_aggr(stat(i, 12, 14), stat(i, 0, 12)))
                nc.vector.tensor_scalar(stat(i, 14, 15), stat(i, 13, 14), EPS, None, ALU.add).then_inc(var_done, 1)
                v.wait_ge(root_done, i + 1)
                after(nc.vector.reciprocal(stat(i, 16, 17), stat(i, 15, 16)))
                after(nc.vector.tensor_scalar(t, t, stat(i, 12, 13), stat(i, 16, 17), ALU.subtract, ALU.mult))
                after(nc.vector.tensor_tensor(t, t, g_row, ALU.mult))
                nc.vector.tensor_tensor(t, t, beta_row, ALU.add).then_inc(normed, 1)
                if i + 2 < tiles:
                    split_y(i + 2)

        @block.tensor
        def _(pe):
            for i in range(tiles):
                pe.wait_ge(y_ready, i + 1)
                if i >= 3:
                    pe.wait_ge(psum_free, i - 2)
                for k in range(KT):
                    if i == 0:
                        pe.wait_ge(out_w.ready, k + 1)
                    for n, (yt, wt) in enumerate(((m.w_hi, m.h_hi), (m.w_hi, m.h_lo), (m.w_lo, m.h_hi))):
                        for half in range(2):
                            mm = nc.tensor.matmul(m.bank(2 * (i % 3) + half), yt[:, i % 2, k, :],
                                                  wt[:, k, half * 512:half * 512 + 512],
                                                  start=(k == 0 and n == 0), stop=(k == KT - 1 and n == 2))
                mm.then_inc(mm_done, 1)
                if l == 0 and i == 0:
                    pe.wait_ge(cols_in, 32)
                    nc.tensor.transpose(m.psum[:, 6, 0:4 * KT], m.v[0:4 * KT, KT, :], m.ident[0:4 * KT, 0:4 * KT])\
                        .then_inc(cols_turned, 1)


def backbone(nc, x, ctx, cond, w_mod, b_cols, b_gate, w_in, w_out, ln_g, ln_b, rpb, lam, sub_g, ident, rope, masks, out):
    scratch = lambda n, s: nc.dram_tensor(n, s, F32, kind="Internal").ap()
    x1 = scratch("x1", (TOK, D))
    mod_rows = scratch("mod_rows", (2, ROW_PAD + 4 * D))
    toeplitz = scratch("toeplitz", (HEADS, GRID_W, RPB_H, GRID_W))
    y_t = [scratch(f"y_t{l}", (D, TOK)) for l in range(DEPTH)]
    rows0 = lambda t: x[t * P:(t + 1) * P, :] if t < LAT_TILES else ctx[(t - LAT_TILES) * P:(t - LAT_TILES + 1) * P, :]
    rows1 = lambda t: x1[t * P:(t + 1) * P, :]
    with ExitStack() as stack:
        m = Memory(nc, stack)
        bands = stack.enter_context(nc.semaphore("bands"))
        loaded = [[stack.enter_context(nc.semaphore(f"t{l}_loaded{g}")) for g in range(3)] for l in range(DEPTH)]

        p = [Projection(nc, m, stack, l, w_in, rotary=(l == 1)) for l in range(DEPTH)]
        out_w = [OutWeights(nc, m, stack, l, w_out) for l in range(DEPTH)]

        def first_tokens(sp):
            send_for_tokens(sp, m, 0, rows0, loaded[0], range(EARLY_TILES[0]))

        def tokens_back(sp, stored):
            for t in range(EARLY_TILES[1]):
                sp.wait_ge(stored[t % 2], 16 * (t // 2 + 1))
                send_for_tokens(sp, m, 1, rows1, loaded[1], [t])

        modulation(nc, m, stack, w_mod, cond, b_cols, lam, sub_g, ident, rpb, toeplitz, bands, first_tokens)
        load_tokens(nc, m, stack, 0, p[0], rows0, loaded[0])
        neighbourhood(nc, m, stack, p[0], out_w[0], rpb, toeplitz, bands, masks, w_mod, mod_rows, y_t[0])
        project(nc, m, stack, 0, out_w[0], y_t[0], lambda cnd: mod_rows[cnd, ROW_PAD:ROW_PAD + D], mod_rows, b_gate, ln_g, ln_b,
                rows0, rows1, TOK_TILES, tokens_back)
        load_tokens(nc, m, stack, 1, p[1], rows1, loaded[1])
        differential(nc, m, stack, p[1], out_w[1], rope, y_t[1])
        project(nc, m, stack, 1, out_w[1], y_t[1], lambda cnd: mod_rows[cnd, ROW_PAD + 3 * D:ROW_PAD + 4 * D], mod_rows, b_gate, ln_g, ln_b,
                rows1, lambda t: out[t * P:(t + 1) * P, :], LAT_TILES)


def shape_constants():
    ident = np.eye(P, dtype=np.float32)
    n_freq = HD // 4
    inv = np.float32(10000.0) ** (-np.arange(n_freq, dtype=np.float32) / np.float32(n_freq))
    t = np.arange(SEQ)
    pos = np.stack([t // GRID_W, t % GRID_W]).astype(np.float32)
    dim = np.arange(P) % HD
    ang = pos[dim // 32] * inv[dim % 16].astype(np.float32)[:, None]
    sign = np.where(dim % 32 < 16, -1.0, 1.0).astype(np.float32)[:, None]
    rope = np.stack([np.cos(ang), np.sin(ang) * sign], axis=1).astype(np.float32)
    w = np.arange(P) % GRID_W
    start = np.clip(w - WIN_C // 2, 0, GRID_W - WIN_C)[:, None]
    j = np.arange(GRID_W)[None]
    cols = np.where((j >= start) & (j < start + WIN_C), 0.0, NEG).astype(np.float32)
    every = np.repeat(cols[:, None], SLOTS, axis=1)
    inner = np.repeat(cols[:, None], INNER, axis=1)
    inner[:GRID_W, INNER - 1] = NEG
    inner[GRID_W:, 0] = NEG
    masks = np.concatenate([every.reshape(P, -1), inner.reshape(P, -1)], axis=1)
    return ident, rope, np.ascontiguousarray(masks)


def kernel(x, c, ctx, c_ctx, w_mod, b_mod, w_in, w_out, ln_g, ln_b, na_rpb, diff_lambda, diff_subln_g):
    import concourse.bacc as bacc
    from concourse.bass_utils import run_bass_kernel_spmd

    a = np.ascontiguousarray
    ident, rope, masks = shape_constants()
    cond = a(np.stack([np.asarray(c)[0], np.asarray(c_ctx)]).reshape(2, KT, P).transpose(2, 0, 1))
    b_mod = np.asarray(b_mod)
    b_cols = a(b_mod[:, 0:2 * D].reshape(DEPTH, 2 * KT, P).transpose(2, 0, 1))
    arrays = {
        "x": a(np.asarray(x)[0]), "ctx": a(np.asarray(ctx)[0]), "cond": cond, "w_mod": a(np.asarray(w_mod).transpose(1, 0, 2).reshape(D, DEPTH * 3 * D)), "b_cols": b_cols,
        "b_gate": a(b_mod[:, 2 * D:]), "w_in": a(w_in), "w_out": a(w_out), "ln_g": a(ln_g), "ln_b": a(ln_b),
        "rpb": a(np.pad(np.asarray(na_rpb)[0], ((0, 0), (0, 0), (PAD, PAD)))),
        "lam": a(np.asarray(diff_lambda)[0].reshape(-1)), "sub_g": a(np.asarray(diff_subln_g)[0].reshape(P, 1)),
        "ident": ident, "rope": rope, "masks": masks,
    }
    nc = bacc.Bacc("TRN2", target_bir_lowering=False, num_devices=1)
    args = [nc.dram_tensor("in_" + n, v.shape, mybir.dt.from_np(v.dtype), kind="ExternalInput").ap() for n, v in arrays.items()]
    out = nc.dram_tensor("out", (SEQ, D), F32, kind="ExternalOutput").ap()
    backbone(nc, *args, out)
    r = run_bass_kernel_spmd(nc, [{"in_" + n: v for n, v in arrays.items()}], core_ids=[0])
    return r.results[0]["out"].reshape(1, SEQ, D)
```
